# Optimizing a Trainium2 kernel written in Bass

```python
import math
import jax, jax.numpy as jnp
from jax import lax
import numpy as np

D_MODEL = 1024
BATCH = 1
SEQ = 256
DEPTH = 2

N_A_LAYERS = (DEPTH + 1) // 2
N_B_LAYERS = DEPTH - N_A_LAYERS
HEAD_DIM = 64
N_HEADS = D_MODEL // HEAD_DIM
N_KV = 4
GQA_R = N_HEADS // N_KV
KV_DIM = N_KV * HEAD_DIM
NUM_BUCKETS = 32
MAX_DISTANCE = 2048
CMP_BLOCK = 32
CMP_STRIDE = 16
CMP_HIDDEN = 256
SEL_BLOCK = 64
SEL_TOPN = 8
SEL_Q_CHUNK = 16
FORCE_BONUS = 100.0
WIN = 256
BAND_BLOCK = 128
DILATIONS = ((128, 1), (512, 4), (2048, 16))
N_DIL = len(DILATIONS)
FFN_HIDDEN = -(-8 * D_MODEL // (3 * 256)) * 256
RMS_EPS = 1e-6
NEG_INF = -1e30
A_IN_DIM = D_MODEL + 6 * KV_DIM + 3 * N_HEADS
B_Q_DIM = N_DIL * D_MODEL
SHARED_KV_DIM = N_DIL * 2 * KV_DIM


def rmsnorm(x, g):
    x32 = x.astype(jnp.float32)
    y = x32 * lax.rsqrt(jnp.mean(x32 * x32, axis=-1, keepdims=True) + RMS_EPS)
    return (y * g.astype(jnp.float32)).astype(x.dtype)

def t5_bucket(dist):
    max_exact = NUM_BUCKETS // 2
    d = jnp.maximum(dist, 0)
    log_ratio = jnp.log(jnp.maximum(d, max_exact).astype(jnp.float32) / max_exact) / math.log(MAX_DISTANCE / max_exact)
    large = max_exact + (log_ratio * (NUM_BUCKETS - max_exact)).astype(jnp.int32)
    return jnp.where(d < max_exact, d, jnp.minimum(large, NUM_BUCKETS - 1))

def masked_softmax(s, mask):
    s = jnp.where(mask, s.astype(jnp.float32), NEG_INF)
    m = jnp.max(s, axis=-1, keepdims=True)
    p = jnp.where(mask, jnp.exp(s - m), 0.0)
    return p, jnp.sum(p, axis=-1, keepdims=True), m

def banded_attention(q, k, v, max_dist, dist_scale, rel_bias):
    n, L, G, R, dh = q.shape
    nb = L // BAND_BLOCK
    n_prev = -(-max_dist // BAND_BLOCK)
    pad = n_prev * BAND_BLOCK
    kw_len = (n_prev + 1) * BAND_BLOCK

    def windows(t):
        tp = jnp.pad(t, ((0, 0), (pad, 0), (0, 0), (0, 0))).reshape(n, nb + n_prev, BAND_BLOCK, G, dh)
        return jnp.concatenate([tp[:, j:j + nb] for j in range(n_prev + 1)], axis=2)

    kw, vw = windows(k), windows(v)
    qb = q.reshape(n, nb, BAND_BLOCK, G, R, dh)
    s = jnp.einsum('nbqgrd,nbkgd->nbgrqk', qb, kw).astype(jnp.float32) * dh ** -0.5
    qi = jnp.arange(BAND_BLOCK)[:, None]
    ki = jnp.arange(kw_len)[None, :]
    dist = pad + qi - ki
    key_pos = jnp.arange(nb)[:, None, None] * BAND_BLOCK - pad + ki[None]
    mask = (dist >= 0) & (dist <= max_dist) & (key_pos >= 0)
    bias = rel_bias[t5_bucket(dist * dist_scale)].reshape(BAND_BLOCK, kw_len, G, R).transpose(2, 3, 0, 1)
    p, denom, m = masked_softmax(s + bias, mask[None, :, None, None])
    o = jnp.einsum('nbgrqk,nbkgd->nbqgrd', p, vw.astype(jnp.float32))
    o = o / denom[..., 0].transpose(0, 1, 4, 2, 3)[..., None]
    lse = (jnp.log(denom) + m)[..., 0].transpose(0, 1, 4, 2, 3).reshape(n, L, G, R)
    return o.reshape(n, L, G, R, dh), lse

def dilated_group_attention(q, k, v, dilation, window, rel_bias):
    B, S = q.shape[:2]
    L = S // dilation
    Lp = -(-L // BAND_BLOCK) * BAND_BLOCK

    def to_sub(t):
        rest = t.shape[2:]
        t = t.reshape((B, L, dilation) + rest)
        t = jnp.moveaxis(t, 2, 1).reshape((B * dilation, L) + rest)
        return jnp.pad(t, ((0, 0), (0, Lp - L)) + ((0, 0),) * len(rest))

    def from_sub(t):
        rest = t.shape[2:]
        t = t[:, :L].reshape((B, dilation, L) + rest)
        return jnp.moveaxis(t, 1, 2).reshape((B, S) + rest)

    o, lse = banded_attention(to_sub(q), to_sub(k), to_sub(v), window // dilation, dilation, rel_bias)
    return from_sub(o), from_sub(lse)

def nsa_attention(h, w_in, b_gate, pe_k, w1_k, w2_k, pe_v, w1_v, w2_v, w_out, rel_bias):
    B, S, _ = h.shape
    proj = h @ w_in
    splits = [D_MODEL + i * KV_DIM for i in range(7)]
    q, kc, vc, ks, vs, kwn, vwn, gl = jnp.split(proj, splits, axis=-1)
    q = q.reshape(B, S, N_KV, GQA_R, HEAD_DIM)
    kvh = lambda t: t.reshape(B, S, N_KV, HEAD_DIM)
    scale = HEAD_DIM ** -0.5
    t_pos = jnp.arange(S)

    n_c = (S - CMP_BLOCK) // CMP_STRIDE + 1
    starts = jnp.arange(n_c) * CMP_STRIDE
    tok_idx = starts[:, None] + jnp.arange(CMP_BLOCK)[None, :]

    def compress(t, pe, w1, w2):
        blk = t[:, tok_idx] + pe[:, None, :]
        blk = jnp.moveaxis(blk, 3, 2).reshape(B, n_c, N_KV, CMP_BLOCK * HEAD_DIM)
        return jax.nn.gelu(blk @ w1) @ w2

    k_cmp = compress(kvh(kc), pe_k, w1_k, w2_k)
    v_cmp = compress(kvh(vc), pe_v, w1_v, w2_v)
    dist_c = t_pos[:, None] - (starts + CMP_BLOCK - 1)[None, :]
    bias_c = rel_bias[t5_bucket(dist_c)].reshape(S, n_c, N_KV, GQA_R).transpose(2, 3, 0, 1)
    s = jnp.einsum('bsgrd,bngd->bgrsn', q, k_cmp).astype(jnp.float32) * scale
    p, denom, _ = masked_softmax(s + bias_c, dist_c >= 0)
    p_cmp = p / jnp.maximum(denom, 1e-30)
    o_cmp = jnp.einsum('bgrsn,bngd->bsgrd', p_cmp, v_cmp.astype(jnp.float32))

    n_sel = S // SEL_BLOCK
    top_n = min(SEL_TOPN, n_sel)
    ci = jnp.arange(n_c)[:, None] * CMP_STRIDE
    sj = jnp.arange(n_sel)[None, :] * SEL_BLOCK
    overlap = ((ci < sj + SEL_BLOCK) & (ci + CMP_BLOCK > sj)).astype(jnp.float32)
    imp = jnp.einsum('bgrsn,nj->bgsj', p_cmp, overlap)
    blk_j = jnp.arange(n_sel)[None, :]
    cur = (t_pos // SEL_BLOCK)[:, None]
    forced = (blk_j == 0) | (blk_j == cur) | (blk_j == cur - 1)
    score = jnp.where(forced, imp + FORCE_BONUS, jnp.where(blk_j <= cur, imp, -1.0))
    _, sel_idx = lax.top_k(score, top_n)

    k_blocks = kvh(ks).reshape(B, n_sel, SEL_BLOCK, N_KV, HEAD_DIM).transpose(0, 3, 1, 2, 4)
    v_blocks = kvh(vs).reshape(B, n_sel, SEL_BLOCK, N_KV, HEAD_DIM).transpose(0, 3, 1, 2, 4)
    n_chunk = S // SEL_Q_CHUNK
    q_ch = jnp.moveaxis(q.reshape(B, n_chunk, SEL_Q_CHUNK, N_KV, GQA_R, HEAD_DIM), 1, 0)
    idx_ch = jnp.moveaxis(sel_idx.reshape(B, N_KV, n_chunk, SEL_Q_CHUNK, top_n), 2, 0)
    c0 = jnp.arange(n_chunk) * SEL_Q_CHUNK
    b_ix = jnp.arange(B)[:, None, None, None]
    g_ix = jnp.arange(N_KV)[None, :, None, None]
    rb_g = rel_bias.reshape(NUM_BUCKETS, N_KV, GQA_R).transpose(1, 0, 2)
    n_keys = top_n * SEL_BLOCK

    def sel_chunk(args):
        qc, ic, start = args
        kg = k_blocks[b_ix, g_ix, ic].reshape(B, N_KV, SEL_Q_CHUNK, n_keys, HEAD_DIM)
        vg = v_blocks[b_ix, g_ix, ic].reshape(B, N_KV, SEL_Q_CHUNK, n_keys, HEAD_DIM)
        kpos = (ic[..., None] * SEL_BLOCK + jnp.arange(SEL_BLOCK)).reshape(B, N_KV, SEL_Q_CHUNK, n_keys)
        dist = (start + jnp.arange(SEL_Q_CHUNK))[:, None] - kpos
        bias = jnp.moveaxis(rb_g[g_ix, t5_bucket(dist)], -1, 3)
        s_sel = jnp.einsum('bcgrd,bgckd->bgcrk', qc, kg).astype(jnp.float32) * scale + bias
        p_sel, den, _ = masked_softmax(s_sel, (dist >= 0)[:, :, :, None, :])
        return jnp.einsum('bgcrk,bgckd->bcgrd', p_sel / jnp.maximum(den, 1e-30), vg.astype(jnp.float32))

    o_sel = jnp.moveaxis(lax.map(sel_chunk, (q_ch, idx_ch, c0)), 0, 1).reshape(B, S, N_KV, GQA_R, HEAD_DIM)

    o_win, _ = banded_attention(q, kvh(kwn), kvh(vwn), WIN - 1, 1, rel_bias)

    g = jax.nn.sigmoid((gl + b_gate).astype(jnp.float32)).reshape(B, S, N_KV, GQA_R, 3)
    o = g[..., 0:1] * o_cmp + g[..., 1:2] * o_sel + g[..., 2:3] * o_win
    return o.reshape(B, S, D_MODEL).astype(h.dtype) @ w_out

def dilated_attention(h, w_q, k_shared, v_shared, w_out, rel_bias):
    B, S, _ = h.shape
    q = (h @ w_q).reshape(B, S, N_DIL, N_KV, GQA_R, HEAD_DIM)
    outs, lses = [], []
    for gi, (window, dilation) in enumerate(DILATIONS):
        o, lse = dilated_group_attention(q[:, :, gi], k_shared[:, :, gi], v_shared[:, :, gi], dilation, window, rel_bias)
        outs.append(o)
        lses.append(lse)
    alpha = jax.nn.softmax(jnp.stack(lses, axis=-1), axis=-1)
    o = jnp.einsum('bsgrdi,bsgri->bsgrd', jnp.stack(outs, axis=-1), alpha)
    return o.reshape(B, S, D_MODEL).astype(h.dtype) @ w_out

def swiglu(h, w_up, w_down):
    a, b = jnp.split(h @ w_up, 2, axis=-1)
    return (jax.nn.silu(a) * b) @ w_down

def first_inputs(seed: int = 0) -> dict:
    key = jax.random.key(seed)
    ks = jax.random.split(key, 20)
    f32 = jnp.float32
    nrm = lambda k, shape, s: s * jax.random.normal(k, shape, f32)
    w = lambda k, shape, fan_in: jax.random.normal(k, shape, f32) * fan_in ** -0.5
    gain = lambda k, shape: 1.0 + 0.05 * jax.random.normal(k, shape, f32)
    cmp_in = CMP_BLOCK * HEAD_DIM
    return {
        "x": jax.random.normal(ks[0], (BATCH, SEQ, D_MODEL), f32),
        "rel_bias": nrm(ks[1], (NUM_BUCKETS, N_HEADS), 0.5),
        "norm_mix": gain(ks[2], (DEPTH, D_MODEL)),
        "norm_ffn": gain(ks[3], (DEPTH, D_MODEL)),
        "a_w_in": w(ks[4], (N_A_LAYERS, D_MODEL, A_IN_DIM), D_MODEL),
        "a_b_gate": nrm(ks[5], (N_A_LAYERS, 3 * N_HEADS), 0.1),
        "a_pe_k": nrm(ks[6], (N_A_LAYERS, CMP_BLOCK, HEAD_DIM), 0.1),
        "a_w1_k": w(ks[7], (N_A_LAYERS, cmp_in, CMP_HIDDEN), cmp_in),
        "a_w2_k": w(ks[8], (N_A_LAYERS, CMP_HIDDEN, HEAD_DIM), CMP_HIDDEN),
        "a_pe_v": nrm(ks[9], (N_A_LAYERS, CMP_BLOCK, HEAD_DIM), 0.1),
        "a_w1_v": w(ks[10], (N_A_LAYERS, cmp_in, CMP_HIDDEN), cmp_in),
        "a_w2_v": w(ks[11], (N_A_LAYERS, CMP_HIDDEN, HEAD_DIM), CMP_HIDDEN),
        "a_w_out": w(ks[12], (N_A_LAYERS, D_MODEL, D_MODEL), D_MODEL),
        "kv_norm": gain(ks[13], (D_MODEL,)),
        "kv_w": w(ks[14], (D_MODEL, SHARED_KV_DIM), D_MODEL),
        "b_w_q": w(ks[15], (N_B_LAYERS, D_MODEL, B_Q_DIM), D_MODEL),
        "b_w_out": w(ks[16], (N_B_LAYERS, D_MODEL, D_MODEL), D_MODEL),
        "ffn_w_up": w(ks[17], (DEPTH, D_MODEL, 2 * FFN_HIDDEN), D_MODEL),
        "ffn_w_down": w(ks[18], (DEPTH, FFN_HIDDEN, D_MODEL), FFN_HIDDEN),
        "final_norm": gain(ks[19], (D_MODEL,)),
    }

def first_block(x, rel_bias, norm_mix, norm_ffn, a_w_in, a_b_gate, a_pe_k, a_w1_k, a_w2_k, a_pe_v, a_w1_v, a_w2_v,
              a_w_out, kv_norm, kv_w, b_w_q, b_w_out, ffn_w_up, ffn_w_down, final_norm):
    B, S, _ = x.shape
    k_shared = v_shared = None
    for layer in range(DEPTH):
        h = rmsnorm(x, norm_mix[layer])
        if layer < N_A_LAYERS:
            i = layer
            mix = nsa_attention(h, a_w_in[i], a_b_gate[i], a_pe_k[i], a_w1_k[i], a_w2_k[i],
                                a_pe_v[i], a_w1_v[i], a_w2_v[i], a_w_out[i], rel_bias)
        else:
            if layer == N_A_LAYERS:
                kv = (rmsnorm(x, kv_norm) @ kv_w).reshape(B, S, N_DIL, 2, N_KV, HEAD_DIM)
                k_shared, v_shared = kv[:, :, :, 0], kv[:, :, :, 1]
            j = layer - N_A_LAYERS
            mix = dilated_attention(h, b_w_q[j], k_shared, v_shared, b_w_out[j], rel_bias)
        x = x + mix.astype(x.dtype)
        x = x + swiglu(rmsnorm(x, norm_ffn[layer]), ffn_w_up[layer], ffn_w_down[layer]).astype(x.dtype)
    return rmsnorm(x, final_norm)


DEPTH_2 = 1

CHUNK = 64
Q_BLOCK = 128
A_HEADS = 8
A_HEAD_DIM = 64
A_WIDTH = A_HEADS * A_HEAD_DIM
IDX_HEADS = 4
IDX_DIM = 64
TOPK_MAX = 256
REL_BUCKETS = 32
REL_MAX_DIST = 128
SSM_GROUPS = 16
SSM_GROUP_CH = 16
SSM_WIDTH = SSM_GROUPS * SSM_GROUP_CH
SSM_STATE = 64
DT_MIN = 0.001
DT_MAX = 0.1
MEM_TOKENS = 256
MEM_HEADS = 4
MEM_HEAD_DIM = 64
MEM_WIDTH = MEM_HEADS * MEM_HEAD_DIM
N_BRANCHES = 3
FFN_DIM = 2816
NORM_EPS = 1e-6
IN_SPLITS = (A_WIDTH, A_HEAD_DIM, A_HEAD_DIM, IDX_HEADS * IDX_DIM, IDX_DIM, IDX_HEADS,
             SSM_WIDTH, MEM_WIDTH, N_BRANCHES * D_MODEL)
W_IN_COLS = (A_WIDTH + 2 * A_HEAD_DIM + IDX_HEADS * IDX_DIM + IDX_DIM + IDX_HEADS
             + SSM_WIDTH + MEM_WIDTH + N_BRANCHES * D_MODEL)


def rms_norm(x, g):
    xf = x.astype(jnp.float32)
    y = xf * lax.rsqrt(jnp.mean(xf * xf, axis=-1, keepdims=True) + NORM_EPS)
    return (y * g.astype(jnp.float32)).astype(x.dtype)

def swiglu_ffn(h, w_in, w_out):
    gate, up = jnp.split(h @ w_in, 2, axis=-1)
    return (jax.nn.silu(gate) * up) @ w_out

def t5_bucket_2(rel):
    half = REL_BUCKETS // 2
    max_exact = half // 2
    n = jnp.abs(rel)
    nf = jnp.maximum(n, 1).astype(jnp.float32)
    large = max_exact + (jnp.log(nf / max_exact) / math.log(REL_MAX_DIST / max_exact)
                         * (half - max_exact)).astype(jnp.int32)
    large = jnp.minimum(large, half - 1)
    return jnp.where(rel > 0, half, 0) + jnp.where(n < max_exact, n, large)

def indexed_sparse_attention(q, k, v, q_idx, k_idx, w_idx, rel_bias):
    b_, s_ = q.shape[0], q.shape[1]
    topk = min(TOPK_MAX, s_ // 4)
    nblk = s_ // Q_BLOCK
    key_pos = jnp.arange(s_, dtype=jnp.int32)
    scale = A_HEAD_DIM ** -0.5
    idx_scale = IDX_DIM ** -0.5
    head_w_scale = IDX_HEADS ** -0.5

    def to_blocks(a):
        return a.reshape((b_, nblk, Q_BLOCK) + a.shape[2:]).swapaxes(0, 1)

    def block(args):
        qb, qib, wb, start = args
        t = start + jnp.arange(Q_BLOCK, dtype=jnp.int32)
        limit = (t // CHUNK + 1) * CHUNK
        rel = jax.nn.relu(jnp.einsum('bqhd,bsd->bqhs', qib, k_idx).astype(jnp.float32) * idx_scale)
        score = jnp.einsum('bqhs,bqh->bqs', rel, wb.astype(jnp.float32) * head_w_scale)
        score = jnp.where(key_pos[None, None, :] < limit[None, :, None], score, -jnp.inf)
        _, sel = lax.top_k(score, topk)
        valid = sel < limit[None, :, None]
        flat = sel.reshape(b_, Q_BLOCK * topk, 1)
        k_sel = jnp.take_along_axis(k, flat, axis=1).reshape(b_, Q_BLOCK, topk, A_HEAD_DIM)
        v_sel = jnp.take_along_axis(v, flat, axis=1).reshape(b_, Q_BLOCK, topk, A_HEAD_DIM)
        bias = rel_bias[t5_bucket_2(sel - t[None, :, None])]
        logits = (jnp.einsum('bqhd,bqkd->bqhk', qb, k_sel).astype(jnp.float32) * scale
                  + jnp.transpose(bias, (0, 1, 3, 2)).astype(jnp.float32))
        logits = jnp.where(valid[:, :, None, :], logits, -jnp.inf)
        p = jax.nn.softmax(logits, axis=-1).astype(v_sel.dtype)
        return jnp.einsum('bqhk,bqkd->bqhd', p, v_sel)

    starts = jnp.arange(nblk, dtype=jnp.int32) * Q_BLOCK
    out = lax.map(block, (to_blocks(q), to_blocks(q_idx), to_blocks(w_idx), starts))
    return out.swapaxes(0, 1).reshape(b_, s_, A_WIDTH)

def _complex_affine_combine(e1, e2):
    a1r, a1i, b1r, b1i = e1
    a2r, a2i, b2r, b2i = e2
    return (a2r * a1r - a2i * a1i,
            a2r * a1i + a2i * a1r,
            a2r * b1r - a2i * b1i + b2r,
            a2r * b1i + a2i * b1r + b2i)

def s5_layer(u, lam_re, lam_im, log_dt, b_re, b_im, c_re, c_im, d):
    b_, s_ = u.shape[0], u.shape[1]
    f32 = jnp.float32
    uf = u.astype(f32).reshape(b_, s_, SSM_GROUPS, SSM_GROUP_CH)
    lr, li = lam_re.astype(f32), lam_im.astype(f32)
    dt = jnp.exp(log_dt.astype(f32))[:, None]
    mag = jnp.exp(lr * dt)
    ar, ai = mag * jnp.cos(li * dt), mag * jnp.sin(li * dt)
    den = lr * lr + li * li
    fr = ((ar - 1.0) * lr + ai * li) / den
    fi = (ai * lr - (ar - 1.0) * li) / den
    br, bi = b_re.astype(f32), b_im.astype(f32)
    bbr = fr[..., None] * br - fi[..., None] * bi
    bbi = fr[..., None] * bi + fi[..., None] * br
    bur = jnp.einsum('bsgc,gpc->bsgp', uf, bbr)
    bui = jnp.einsum('bsgc,gpc->bsgp', uf, bbi)
    elems = (jnp.broadcast_to(ar, bur.shape), jnp.broadcast_to(ai, bur.shape), bur, bui)
    _, _, xr, xi = lax.associative_scan(_complex_affine_combine, elems, axis=1)
    y = (jnp.einsum('bsgp,gcp->bsgc', xr, c_re.astype(f32))
         - jnp.einsum('bsgp,gcp->bsgc', xi, c_im.astype(f32))
         + d.astype(f32).reshape(SSM_GROUPS, SSM_GROUP_CH) * uf)
    return y.reshape(b_, s_, SSM_WIDTH).astype(u.dtype)

def memory_attention(q, k, v):
    logits = jnp.einsum('bshd,bmhd->bhsm', q, k).astype(jnp.float32) * (MEM_HEAD_DIM ** -0.5)
    p = jax.nn.softmax(logits, axis=-1).astype(v.dtype)
    out = jnp.einsum('bhsm,bmhd->bshd', p, v)
    return out.reshape(q.shape[0], q.shape[1], MEM_WIDTH)

def second_inputs(seed: int = 0) -> dict:
    key = jax.random.key(seed)
    ks = jax.random.split(key, 32)
    f32 = jnp.float32
    L = DEPTH_2

    def nrm(k, shape, scale):
        return jax.random.normal(k, shape, f32) * scale

    def gain(k, shape):
        return 1.0 + 0.02 * jax.random.normal(k, shape, f32)

    n = jnp.arange(SSM_STATE, dtype=f32)
    return {
        'x': nrm(ks[0], (BATCH, SEQ, D_MODEL), 1.0),
        'mem': nrm(ks[1], (BATCH, MEM_TOKENS, D_MODEL), 1.0),
        'ffn1_norm': gain(ks[2], (L, D_MODEL)),
        'ffn1_w_in': nrm(ks[3], (L, D_MODEL, 2 * FFN_DIM), D_MODEL ** -0.5),
        'ffn1_w_out': nrm(ks[4], (L, FFN_DIM, D_MODEL), FFN_DIM ** -0.5),
        'mix_norm': gain(ks[5], (L, D_MODEL)),
        'w_in': nrm(ks[6], (L, D_MODEL, W_IN_COLS), D_MODEL ** -0.5),
        'a_q_gain': gain(ks[7], (L, A_HEAD_DIM)),
        'a_k_gain': gain(ks[8], (L, A_HEAD_DIM)),
        'rel_bias': nrm(ks[9], (REL_BUCKETS, A_HEADS), 0.5),
        'w_o_a': nrm(ks[10], (L, A_WIDTH, D_MODEL), A_WIDTH ** -0.5),
        'ssm_lambda_re': -0.5 + nrm(ks[11], (L, SSM_GROUPS, SSM_STATE), 0.01),
        'ssm_lambda_im': math.pi * n + nrm(ks[12], (L, SSM_GROUPS, SSM_STATE), 0.01),
        'ssm_log_dt': jax.random.uniform(ks[13], (L, SSM_GROUPS), f32,
                                         minval=math.log(DT_MIN), maxval=math.log(DT_MAX)),
        'ssm_b_re': nrm(ks[14], (L, SSM_GROUPS, SSM_STATE, SSM_GROUP_CH), (2 * SSM_GROUP_CH) ** -0.5),
        'ssm_b_im': nrm(ks[15], (L, SSM_GROUPS, SSM_STATE, SSM_GROUP_CH), (2 * SSM_GROUP_CH) ** -0.5),
        'ssm_c_re': nrm(ks[16], (L, SSM_GROUPS, SSM_GROUP_CH, SSM_STATE), SSM_STATE ** -0.5),
        'ssm_c_im': nrm(ks[17], (L, SSM_GROUPS, SSM_GROUP_CH, SSM_STATE), SSM_STATE ** -0.5),
        'ssm_d': nrm(ks[18], (L, SSM_WIDTH), 1.0),
        'w_glu': nrm(ks[19], (L, SSM_WIDTH, 2 * D_MODEL), SSM_WIDTH ** -0.5),
        'mem_norm': gain(ks[20], (L, D_MODEL)),
        'w_mem_kv': nrm(ks[21], (L, D_MODEL, 2 * MEM_WIDTH), D_MODEL ** -0.5),
        'm_q_gain': gain(ks[22], (L, MEM_HEAD_DIM)),
        'm_k_gain': gain(ks[23], (L, MEM_HEAD_DIM)),
        'w_o_m': nrm(ks[24], (L, MEM_WIDTH, D_MODEL), MEM_WIDTH ** -0.5),
        'w_out': nrm(ks[25], (L, D_MODEL, D_MODEL), D_MODEL ** -0.5),
        'ffn2_norm': gain(ks[26], (L, D_MODEL)),
        'ffn2_w_in': nrm(ks[27], (L, D_MODEL, 2 * FFN_DIM), D_MODEL ** -0.5),
        'ffn2_w_out': nrm(ks[28], (L, FFN_DIM, D_MODEL), FFN_DIM ** -0.5),
        'final_norm': gain(ks[29], (L, D_MODEL)),
    }

def second_block(x, mem, ffn1_norm, ffn1_w_in, ffn1_w_out, mix_norm, w_in, a_q_gain, a_k_gain,
              rel_bias, w_o_a, ssm_lambda_re, ssm_lambda_im, ssm_log_dt, ssm_b_re, ssm_b_im,
              ssm_c_re, ssm_c_im, ssm_d, w_glu, mem_norm, w_mem_kv, m_q_gain, m_k_gain, w_o_m,
              w_out, ffn2_norm, ffn2_w_in, ffn2_w_out, final_norm):
    b_, s_ = x.shape[0], x.shape[1]
    offsets = [sum(IN_SPLITS[:i + 1]) for i in range(len(IN_SPLITS) - 1)]
    for l in range(DEPTH_2):
        x = x + 0.5 * swiglu_ffn(rms_norm(x, ffn1_norm[l]), ffn1_w_in[l], ffn1_w_out[l])
        h = rms_norm(x, mix_norm[l])
        q_a, k_a, v_a, q_i, k_i, w_i, u_s, q_m, gates = jnp.split(h @ w_in[l], offsets, axis=-1)
        q_a = rms_norm(q_a.reshape(b_, s_, A_HEADS, A_HEAD_DIM), a_q_gain[l])
        k_a = rms_norm(k_a, a_k_gain[l])
        o_a = indexed_sparse_attention(q_a, k_a, v_a, q_i.reshape(b_, s_, IDX_HEADS, IDX_DIM),
                                       k_i, w_i, rel_bias) @ w_o_a[l]
        y_s = jax.nn.gelu(s5_layer(u_s, ssm_lambda_re[l], ssm_lambda_im[l], ssm_log_dt[l],
                                   ssm_b_re[l], ssm_b_im[l], ssm_c_re[l], ssm_c_im[l], ssm_d[l]))
        glu_a, glu_b = jnp.split(y_s @ w_glu[l], 2, axis=-1)
        o_b = glu_a * jax.nn.sigmoid(glu_b)
        mem_kv = rms_norm(mem, mem_norm[l]) @ w_mem_kv[l]
        m_k, m_v = jnp.split(mem_kv, 2, axis=-1)
        m_k = rms_norm(m_k.reshape(b_, MEM_TOKENS, MEM_HEADS, MEM_HEAD_DIM), m_k_gain[l])
        m_v = m_v.reshape(b_, MEM_TOKENS, MEM_HEADS, MEM_HEAD_DIM)
        q_m = rms_norm(q_m.reshape(b_, s_, MEM_HEADS, MEM_HEAD_DIM), m_q_gain[l])
        o_m = memory_attention(q_m, m_k, m_v) @ w_o_m[l]
        g = jax.nn.sigmoid(gates.reshape(b_, s_, N_BRANCHES, D_MODEL))
        merged = g[:, :, 0] * o_a + g[:, :, 1] * o_b + g[:, :, 2] * o_m
        x = x + merged @ w_out[l]
        x = x + 0.5 * swiglu_ffn(rms_norm(x, ffn2_norm[l]), ffn2_w_in[l], ffn2_w_out[l])
        x = rms_norm(x, final_norm[l])
    return x


def setup_inputs(seed=0):
    out = dict(first_inputs(seed))
    for name, value in second_inputs(seed + 1).items():
        if name != "x":
            out[name + "_2"] = value
    return out


def reference(
    x, rel_bias, norm_mix, norm_ffn, a_w_in, a_b_gate, a_pe_k, a_w1_k, a_w2_k, a_pe_v, a_w1_v,
    a_w2_v, a_w_out, kv_norm, kv_w, b_w_q, b_w_out, ffn_w_up, ffn_w_down, final_norm, mem_2,
    ffn1_norm_2, ffn1_w_in_2, ffn1_w_out_2, mix_norm_2, w_in_2, a_q_gain_2, a_k_gain_2,
    rel_bias_2, w_o_a_2, ssm_lambda_re_2, ssm_lambda_im_2, ssm_log_dt_2, ssm_b_re_2, ssm_b_im_2,
    ssm_c_re_2, ssm_c_im_2, ssm_d_2, w_glu_2, mem_norm_2, w_mem_kv_2, m_q_gain_2, m_k_gain_2,
    w_o_m_2, w_out_2, ffn2_norm_2, ffn2_w_in_2, ffn2_w_out_2, final_norm_2,
):
    x = first_block(
        x, rel_bias, norm_mix, norm_ffn, a_w_in, a_b_gate, a_pe_k, a_w1_k, a_w2_k, a_pe_v,
        a_w1_v, a_w2_v, a_w_out, kv_norm, kv_w, b_w_q, b_w_out, ffn_w_up, ffn_w_down,
        final_norm,
    )
    return second_block(
        x, mem_2, ffn1_norm_2, ffn1_w_in_2, ffn1_w_out_2, mix_norm_2, w_in_2, a_q_gain_2,
        a_k_gain_2, rel_bias_2, w_o_a_2, ssm_lambda_re_2, ssm_lambda_im_2, ssm_log_dt_2,
        ssm_b_re_2, ssm_b_im_2, ssm_c_re_2, ssm_c_im_2, ssm_d_2, w_glu_2, mem_norm_2,
        w_mem_kv_2, m_q_gain_2, m_k_gain_2, w_o_m_2, w_out_2, ffn2_norm_2, ffn2_w_in_2,
        ffn2_w_out_2, final_norm_2,
    )


_drawn_inputs = setup_inputs


def setup_inputs(seed=0):
    import zlib

    import numpy as np

    out = dict(_drawn_inputs(seed))
    spreads = {}
    factors = {'a_b_gate': 2.858,
     'a_pe_k': 4.849,
     'kv_norm': 2.996,
     'ffn1_norm_2': 4.311,
     'mix_norm_2': 3.569,
     'a_q_gain_2': 8.0,
     'a_k_gain_2': 8.0,
     'ssm_lambda_re_2': 64.0,
     'ssm_lambda_im_2': 27.008,
     'ssm_log_dt_2': 29.76,
     'ssm_b_re_2': 38.496,
     'ssm_b_im_2': 37.824,
     'ssm_c_re_2': 39.936,
     'ssm_c_im_2': 36.856,
     'mem_norm_2': 8.0,
     'm_q_gain_2': 8.0,
     'm_k_gain_2': 8.0,
     'ffn2_norm_2': 7.12,
     'final_norm_2': 7.801,
     'rel_bias_2': 3.456}
    for name, (base, spread) in spreads.items():
        noise = np.random.default_rng([zlib.crc32(name.encode()), seed]).standard_normal(out[name].shape)
        drawn = base * np.exp(spread * noise) if base else spread * noise
        out[name] = __import__('jax').numpy.asarray(drawn.astype(out[name].dtype))
    for name, factor in factors.items():
        out[name] = (out[name] * factor).astype(out[name].dtype)
    return out
```

```python
from contextlib import ExitStack
import math

import numpy as np
import concourse.bass as bass
from concourse import mybir

F32 = mybir.dt.float32
F32R = mybir.dt.float32r
ALU = mybir.AluOpType
ACT = mybir.ActivationFunctionType
AX_X = mybir.AxisListType.X

class Names:
    pass


P = 128
D = 1024
S = 256
TT = S // P
KT = D // P
FH = 2816
FSTEP = 256
NSTEP = FH // FSTEP
HEADS = 16
KV = 4
DH = 64
EPS = 1e-6
NEG = -1e30
NCMP = (S - 32) // 16 + 1
IDX_TOPK = 64
ULEN = 2048
TR_BANK, DOWN_BANK = 2, 4
MASKED, TAKEN = -3.0e38, -3.3e38

W_NAT, W_G0, W_G1, W_G2 = 383, 511, 255, 255
O_NAT, O_G0 = 0, W_NAT
O_G1, O_G2 = O_G0 + W_G0, O_G0 + W_G0 + W_G1
W_ALL = O_G2 + W_G2
W_IDX = 383


def bucket_causal(dist):
    d = np.maximum(dist, 0)
    ratio = np.log(np.maximum(d, 16).astype(np.float32) / np.float32(16)) / np.float32(math.log(2048 / 16))
    return np.where(d < 16, d, np.minimum(16 + (ratio * np.float32(16)).astype(np.int32), 31))


def bucket_both_ways(rel):
    n = np.abs(rel)
    ratio = np.log(np.maximum(n, 1).astype(np.float32) / np.float32(8)) / np.float32(math.log(128 / 8))
    large = np.minimum(8 + (ratio * np.float32(8)).astype(np.int32), 15)
    return np.where(rel > 0, 16, 0) + np.where(n < 8, n, large)


def shape_constants():
    def one_hot(dist, ok, fn, rows):
        t = np.zeros((rows, len(dist)), np.float32)
        t[np.where(ok, fn(dist), rows - 1), np.arange(len(dist))] = 1.0
        return t
    nat = 255 - np.arange(W_NAT)
    g0 = 255 - np.arange(W_G0)
    g1 = 127 - np.arange(W_G1)
    g2 = 127 - np.arange(W_G2)
    hot = np.concatenate([
        one_hot(nat, nat >= 0, bucket_causal, 33),
        one_hot(g0, (g0 >= 0) & (g0 <= 128), bucket_causal, 33),
        one_hot(2 * g1, (g1 >= 0) & (g1 % 2 == 0), bucket_causal, 33),
        one_hot(2 * g2, (g2 >= 0) & (g2 % 8 == 0), bucket_causal, 33)], axis=1)
    rel = np.arange(W_IDX) - 255
    hot_idx = one_hot(rel, rel < 10000, bucket_both_ways, 32)
    i = np.arange(P)
    parity = np.stack([(i // 16 + 1) % 2, (i // 16) % 2], axis=1).astype(np.float32)
    ones64 = (i[:, None] // DH == i[None, :] // DH).astype(np.float32)
    return {"c_ident": np.eye(P, dtype=np.float32), "c_hot": hot, "c_hot_idx": hot_idx,
            "c_parity": parity, "c_ones64": ones64}



def slot(n):
    return n % 3


def plan_units():
    units = []
    def block(stage, cols=512):
        units.extend([(stage, 1, 4 * cols)] * 2)
    def ffn(r):
        units.extend([(f"ffn{r}", 2, ULEN)] * 4)
        for _ in range(NSTEP - 2):
            units.extend([(f"ffn{r}", 1, ULEN), (f"ffn{r}", 2, ULEN), (f"ffn{r}", 2, ULEN)])
        units.extend([(f"ffn{r}", 1, ULEN)] * 2)
    for _ in range(5):
        block("a_in")
    units.append(("a_in", 1, KT * 48))
    units.extend([("a_out", 2, ULEN)] * 4)
    ffn(0)
    for _ in range(3 + 6):
        block("b_in")
    units.extend([("b_out", 2, ULEN)] * 4)
    ffn(1)
    ffn(2)
    block("mem_kv")
    for _ in range(3):
        block("c_in")
    for _ in range(2):
        block("merge")
        units.append(("merge", 1, ULEN))
        block("merge")
        units.append(("merge", 2, ULEN))
        block("merge")
        units.append(("merge", 1, ULEN // 2))
    for _ in range(2):
        block("c_out")
    ffn(3)
    return units


UNITS = plan_units()


PAIRED = {"a_in": range(0, 4), "b_in": range(6, 18)}


def paired(n):
    stage = UNITS[n][0]
    return stage in PAIRED and n - first_unit(stage) in PAIRED[stage]


def split_views(m, n, w):
    views = [buf[:, slot(n), 0:w] for buf in (m.WH, m.WL, m.RAW)]
    if paired(n):
        views[0] = views[0].rearrange("p (r x d) -> p r x d", r=4, d=DH)
        views[1] = views[1].rearrange("p (r x d) -> p r x d", r=4, d=DH)
        views[2] = views[2].rearrange("p (x r d) -> p r x d", r=4, d=DH)
    return views


def first_unit(stage):
    return [n for n, u in enumerate(UNITS) if u[0] == stage][0]


def landed_value(n):
    return 16 * sum(u[1] for i, u in enumerate(UNITS[:n + 1]) if slot(i) == slot(n))


def load_unit(sp, m, n, parts):
    if n >= 3:
        sp.wait_ge(m.lo_done, n - 2)
    assert len(parts) == UNITS[n][1], (n, UNITS[n])
    for dst, src in parts:
        sp.dma_start(dst, src).then_inc(m.raw_landed[slot(n)], 16)


def split_hi(act, m, n):
    w = UNITS[n][2]
    act.wait_ge(m.raw_landed[slot(n)], landed_value(n))
    if n >= 3:
        act.wait_ge(m.unit_used, n - 2)
    hi, _, raw = split_views(m, n, w)
    act.activation(hi, raw, ACT.Copy).then_inc(m.hi_done, 1)


def split_lo(dve, m, n):
    w = UNITS[n][2]
    dve.wait_ge(m.hi_done, n + 1)
    hi, lo, raw = split_views(m, n, w)
    dve.tensor_tensor(lo, raw, hi.bitcast(F32), ALU.subtract).then_inc(m.lo_done, 1)


def split_hi_stage(act, m, stage):
    for n, u in enumerate(UNITS):
        if u[0] == stage:
            split_hi(act, m, n)


def split_lo_stage(dve, m, stage):
    for n, u in enumerate(UNITS):
        if u[0] == stage:
            split_lo(dve, m, n)


def mm3(pe, out, lh, ll, rh, rl, start):
    pe.matmul(out, lh, rh, start=start, stop=False, skip_group_check=True)
    pe.matmul(out, lh, rl, start=False, stop=False, skip_group_check=True)
    return pe.matmul(out, ll, rh, start=False, stop=True, skip_group_check=True)


def mm(pe, out, lhsT, rhs, start, stop=True):
    return pe.matmul(out, lhsT, rhs, start=start, stop=stop, skip_group_check=True)



def norm_squares_scalar(act, m, src, ready, stage):
    if stage:
        split_ahead(act, m, split_hi, stage, 0, 2)
    sem, value, per_tile = ready
    for t in range(TT):
        act.wait_ge(sem, value + per_tile * t)
        act.activation(m.HN[:, t, :], src[:, t, :], ACT.Square,
                       accum_out=m.SS[:, t:t + 1]).then_inc(m.s("norm_squared"), 1)


def norm_turned_scalar(act, m, k, outs, gains=False):
    tr, hi = m.s("norm_transposed"), m.s("norm_hi")
    if gains:
        act.wait_ge(m.s("gains_set"), 1)
    for b in range(4):
        act.wait_ge(tr, 4 * k + b + 1)
        for kt in (2 * b, 2 * b + 1):
            for oh, _, g in outs:
                ins = act.activation(oh[:, kt, :], m.pb[b][:, (kt % 2) * S:(kt % 2 + 1) * S], ACT.Copy,
                                     scale=m.GC[:, g * KT + kt:g * KT + kt + 1])
        ins.then_inc(hi, 1)


def norm_scalar(act, m, k, src, outs, ready, stage, gains=False):
    norm_squares_scalar(act, m, src, ready, stage)
    norm_turned_scalar(act, m, k, outs, gains)


def norm_gpsimd(pool, m, k):
    pool.wait_ge(m.s("norm_mean"), k + 1)
    pool.tensor_tensor(m.RS[:, 0:TT], m.MS[:, 0:TT], m.NEGHALF[:, 0:TT], ALU.pow)\
        .then_inc(m.s("norm_rsqrt"), 1)


def norm_scale_vector(dve, m, k, src):
    sq, mean, rsq, hn = (m.s(f"norm_{x}") for x in ("squared", "mean", "rsqrt", "scaled"))
    dve.wait_ge(sq, TT * (k + 1))
    dve.tensor_scalar(m.MS[:, 0:TT], m.SS[:, 0:TT], 1.0 / D, EPS, ALU.mult, ALU.add).then_inc(mean, 1)
    dve.wait_ge(rsq, k + 1)
    for t in range(TT):
        dve.tensor_scalar(m.HN[:, t, :], src[:, t, :], m.RS[:, t:t + 1], None, ALU.mult).then_inc(hn, 1)


def norm_turned_vector(dve, m, k, outs):
    hi, lo = m.s("norm_hi"), m.s("norm_lo")
    for b in range(4):
        dve.wait_ge(hi, 4 * k + b + 1)
        for kt in (2 * b, 2 * b + 1):
            for oh, ol, g in outs:
                ins = dve.scalar_tensor_tensor(
                    out=ol[:, kt, :], in0=m.pb[b][:, (kt % 2) * S:(kt % 2 + 1) * S],
                    scalar=m.GC[:, g * KT + kt:g * KT + kt + 1], in1=oh[:, kt, :].bitcast(F32),
                    op0=ALU.mult, op1=ALU.subtract)
        ins.then_inc(lo, 1)


def norm_vector(dve, m, k, src, outs):
    norm_scale_vector(dve, m, k, src)
    norm_turned_vector(dve, m, k, outs)


def norm_tensor(pe, m, k):
    pe.wait_ge(m.s("norm_scaled"), TT * (k + 1))
    for b in range(4):
        for kt in (2 * b, 2 * b + 1):
            for t in range(TT):
                ins = pe.transpose(m.pb[b][:, (kt % 2) * S + t * P:(kt % 2) * S + (t + 1) * P],
                                   m.HN[:, t, kt * P:(kt + 1) * P], m.IDENT[:, :])
        ins.then_inc(m.s("norm_transposed"), 1)


def wait_rows(pe, m, k, half):
    pe.wait_ge(m.s("norm_lo"), 4 * k + 2 * half + 2)



def ffn_sync(sp, m, r, w_up, w_down):
    n0 = first_unit(f"ffn{r}")
    up = w_up.rearrange("(k p) (g f) -> p k g f", p=P, g=2)
    down = w_down.rearrange("(f q p) n -> p f q n", p=P, q=2)

    def raw(j):
        return m.RAW[:, slot(j), :].rearrange("p (k g c) -> p k g c", k=4, g=2)

    def up_parts(j, half, s):
        at = bass.ds(s * FSTEP, FSTEP)
        return [(raw(j)[:, :, g, :], up[:, 4 * half:4 * half + 4, g, at]) for g in range(2)]

    def down_parts(j, s):
        return [(m.RAW[:, slot(j), :].rearrange("p (q n) -> p q n", q=2), down[:, bass.ds(s, 1), :, :]
                 .rearrange("p f q n -> p (f q) n"))]

    for s in range(2):
        for half in range(2):
            load_unit(sp, m, n0 + 2 * s + half, up_parts(n0 + 2 * s + half, half, s))
    with sp.Fori(0, NSTEP - 2) as s:
        for j, parts in ((4, down_parts(n0 + 4, s)), (5, up_parts(n0 + 5, 0, s + 2)),
                         (6, up_parts(n0 + 6, 1, s + 2))):
            sp.wait_ge(m.lo_done, n0 + j - 2 + 3 * s)
            for dst, src in parts:
                sp.dma_start(dst, src).then_inc(m.raw_landed[slot(n0 + j)], 16)
    for s in (NSTEP - 2, NSTEP - 1):
        n = n0 + 4 + 3 * (NSTEP - 2) + (s - (NSTEP - 2))
        load_unit(sp, m, n, down_parts(n, s))


def ffn_scalar(act, m, r):
    n0, f0 = first_unit(f"ffn{r}"), r * NSTEP
    up_done, th, tr, hi = (m.s(f"ffn_{x}") for x in ("up0", "tanh", "transposed", "hi"))

    def split(j, s):
        dmas = UNITS[n0 + j][1]
        act.wait_ge(m.raw_landed[slot(n0 + j)], landed_value(n0 + j) + 16 * dmas * s)
        act.wait_ge(m.unit_used, n0 + j - 2 + 3 * s)
        act.activation(m.WH[:, slot(n0 + j), :], m.RAW[:, slot(n0 + j), :], ACT.Copy).then_inc(m.hi_done, 1)

    def gate(s, n):
        act.wait_ge(up_done, s + 1 + f0)
        act.activation(m.TH[:, 0, :], m.pb[0][:, 0:FSTEP], ACT.Tanh, scale=0.5).then_inc(th, 1)
        act.wait_ge(m.unit_used, n)
        act.activation(m.TH[:, 1, :], m.pb[1][:, 0:FSTEP], ACT.Tanh, scale=0.5).then_inc(th, 1)

    def turned_hi(s):
        act.wait_ge(tr, s + 1 + f0)
        act.activation(m.GTH, m.pb[TR_BANK][:, :], ACT.Copy).then_inc(hi, 1)

    split_hi(act, m, n0 + 2)
    gate(0, n0 + 2)
    split_hi(act, m, n0 + 3)
    turned_hi(0)
    split_hi(act, m, n0 + 4)
    split_hi(act, m, n0 + 5)
    gate(1, n0 + 4)
    split_hi(act, m, n0 + 6)
    with act.Fori(0, NSTEP - 3) as s:
        turned_hi(s + 1)
        split(7, s)
        split(8, s)
        gate(s + 2, n0 + 7 + 3 * s)
        split(9, s)
    turned_hi(NSTEP - 2)
    split_hi(act, m, n0 + 31)
    gate(NSTEP - 1, n0 + 31)
    turned_hi(NSTEP - 1)
    split_hi(act, m, n0 + 32)


def ffn_vector(dve, m, r, factor, following=None):
    n0, f0 = first_unit(f"ffn{r}"), r * NSTEP
    th, hi, lo, u, g = (m.s(f"ffn_{x}") for x in ("tanh", "hi", "lo", "silu", "gated"))

    def split(j, s):
        dve.wait_ge(m.hi_done, n0 + j + 1 + 3 * s)
        dve.tensor_tensor(m.WL[:, slot(n0 + j), :], m.RAW[:, slot(n0 + j), :],
                          m.WH[:, slot(n0 + j), :].bitcast(F32), ALU.subtract).then_inc(m.lo_done, 1)

    def gate(s):
        for t in range(TT):
            dve.wait_ge(th, 2 * s + t + 1 + 2 * f0)
            dve.scalar_tensor_tensor(out=m.UU[:, t, :], in0=m.TH[:, t, :], scalar=1.0,
                                     in1=m.pb[t][:, 0:FSTEP], op0=ALU.add, op1=ALU.mult).then_inc(u, 1)
            dve.wait_ge(u, 2 * s + t + 1 + 2 * f0)
            dve.tensor_tensor(m.GG[:, t, :], m.UU[:, t, :], m.pb[t][:, FSTEP:2 * FSTEP], ALU.mult)\
                .then_inc(g, 1)

    def turned_lo(s):
        dve.wait_ge(hi, s + 1 + f0)
        dve.tensor_tensor(m.GTL, m.pb[TR_BANK][:, :], m.GTH.bitcast(F32), ALU.subtract).then_inc(lo, 1)

    split_lo(dve, m, n0 + 2)
    gate(0)
    split_lo(dve, m, n0 + 3)
    turned_lo(0)
    split_lo(dve, m, n0 + 4)
    split_lo(dve, m, n0 + 5)
    gate(1)
    split_lo(dve, m, n0 + 6)
    with dve.Fori(0, NSTEP - 3) as s:
        turned_lo(s + 1)
        split(7, s)
        split(8, s)
        gate(s + 2)
        split(9, s)
    turned_lo(NSTEP - 2)
    split_lo(dve, m, n0 + 31)
    gate(NSTEP - 1)
    turned_lo(NSTEP - 1)
    split_lo(dve, m, n0 + 32)
    if following:
        split_ahead(dve, m, split_lo, following, 0, 2)
    add_residual(dve, m, factor, (1, 3, 4, 6)[r], n0 + 32)


def ffn_tensor(pe, m, r, norm):
    n0, f0 = first_unit(f"ffn{r}"), r * NSTEP
    up_done, g, tr, lo = (m.s(f"ffn_{x}") for x in ("up0", "gated", "transposed", "lo"))

    def up(s, j, e, first=False):
        for half in range(2):
            if first:
                wait_rows(pe, m, norm, half)
            pe.wait_ge(m.lo_done, n0 + j + half + 1 + e)
            sl = slot(n0 + j + half)
            for t in range(TT):
                for k in range(4):
                    kt = 4 * half + k
                    tok = slice(t * P, (t + 1) * P)
                    col = slice(k * 512, (k + 1) * 512)
                    ins = mm3(pe, m.pb[t][:, :], m.HTH[:, kt, tok], m.HTL[:, kt, tok],
                              m.WH[:, sl, col], m.WL[:, sl, col], kt == 0)
                if half == 1 and t == 0:
                    ins.then_inc(up_done, 1)
            ins.then_inc(m.unit_used, 1)

    def turn(s):
        pe.wait_ge(g, 2 * s + 2 + 2 * f0)
        for q in range(2):
            for t in range(TT):
                ins = pe.transpose(m.pb[TR_BANK][:, q * S + t * P:q * S + (t + 1) * P],
                                   m.GG[:, t, q * P:(q + 1) * P], m.IDENT[:, :])
        ins.then_inc(tr, 1)

    def down(s, j, e, start, last=False):
        pe.wait_ge(m.lo_done, n0 + j + 1 + e)
        pe.wait_ge(lo, s + 1 + f0)
        sl = slot(n0 + j)
        for t in range(TT):
            for q in range(2):
                for h in range(2):
                    col = slice(q * D + h * 512, q * D + (h + 1) * 512)
                    tok = slice(q * S + t * P, q * S + (t + 1) * P)
                    ins = mm3(pe, m.pb[DOWN_BANK + 2 * t + h][:, :], m.GTH[:, tok], m.GTL[:, tok],
                              m.WH[:, sl, col], m.WL[:, sl, col], start and q == 0)
            if last and t == 0:
                ins.then_inc(m.s("first_tile_done"), 1)
        ins.then_inc(m.unit_used, 1)

    up(0, 0, 0, first=True)
    turn(0)
    up(1, 2, 0)
    down(0, 4, 0, True)
    turn(1)
    with pe.Fori(0, NSTEP - 2) as s:
        up(s + 2, 5, 3 * s)
        down(s + 1, 7, 3 * s, False)
        turn(s + 2)
    down(NSTEP - 1, 32, 0, False, last=True)


def add_residual(dve, m, factor, k, unit):
    for t in range(TT):
        if t == 0:
            dve.wait_ge(m.s("first_tile_done"), k + 1)
        else:
            dve.wait_ge(m.unit_used, unit + 1)
        for h in range(2):
            x = m.XR[:, t, h * 512:(h + 1) * 512]
            ins = dve.scalar_tensor_tensor(out=x, in0=m.pb[DOWN_BANK + 2 * t + h][:, :], scalar=factor,
                                           in1=x, op0=ALU.mult, op1=ALU.add)
        ins.then_inc(m.x_ready, 1)


N_FIRST = 10


def first_loads_sync(sp, m):
    i = m.i
    sp.dma_start(m.XR[:, :, :], i["x"][0].rearrange("(t p) d -> p t d", p=P)).then_inc(m.s("x_in"), 16)
    loads = [(m.IDENT[:, :], i["c_ident"])]
    gains = [i["norm_mix"][0, :], i["norm_ffn"][0, :], i["kv_norm"], i["norm_mix"][1, :], i["norm_ffn"][1, :],
             i["ffn1_norm_2"][0, :], i["mem_norm_2"][0, :], i["mix_norm_2"][0, :], i["ffn2_norm_2"][0, :]]
    for g, src in enumerate(gains):
        loads.append((m.GROW[g * KT:(g + 1) * KT, :], src.rearrange("(k p) -> k p", p=P)))
    assert len(loads) == N_FIRST
    for dst, src in loads:
        sp.dma_start(dst, src).then_inc(m.s("first_in"), 16)


def setup_dma(pool, m):
    i = m.i
    pool.wait_ge(m.s("mask_row_set"), 1)
    loads = [(m.HOT, i["c_hot"]), (m.HOTI, i["c_hot_idx"]),
             (m.ONES64[:, :], i["c_ones64"]), (m.PAR[:, :], i["c_parity"]),
             (m.RB[0:32, :], i["rel_bias"]), (m.RBI[:, :], i["rel_bias_2"])]
    for n, src in enumerate([i["a_q_gain_2"], i["a_k_gain_2"], i["m_q_gain_2"], i["m_k_gain_2"]]):
        for h in range(2):
            loads.append((m.HG[h * DH:(h + 1) * DH, n:n + 1], src.rearrange("a d -> d a")))
    for n, src in enumerate([i["a_pe_k"], i["a_pe_v"]]):
        for h in range(2):
            loads.append((m.PE[h * DH:(h + 1) * DH, n, :],
                          src.rearrange("a (u h) d -> a h d u", h=2)[0, h]))
    for h in range(2):
        for n, src in enumerate([i["a_w2_k"], i["a_w2_v"]]):
            loads.append((m.W2[:, n, :, h * DH:(h + 1) * DH], src[0].rearrange("(k p) d -> p k d", p=P)))
    loads.append((m.BGATE[:, :], bass.AP(i["a_b_gate"].tensor, 0, [[0, P], [1, 48]])))
    assert len(loads) == m.n_consts, len(loads)
    for dst, src in loads:
        pool.dma_start(dst, src).then_inc(m.consts_in, 16)


def setup_vector(dve, m):
    dve.memset(m.RB[:, :], NEG).then_inc(m.s("mask_row_set"), 1)
    dve.memset(m.NEGHALF[:, 0:2], -0.5).then_inc(m.s("neghalf_set"), 1)
    dve.memset(m.NEGHALF[:, 2:3], -1.0).then_inc(m.s("neghalf_set"), 1)
    dve.wait_ge(m.s("gains_turned"), 1)
    dve.tensor_copy(m.GC[:, :], m.pb[7][:, 0:72]).then_inc(m.s("gains_set"), 1)


def setup_tensor(pe, m):
    pe.wait_ge(m.s("first_in"), 16 * N_FIRST)
    pe.transpose(m.pb[7][:, 0:72], m.GROW[:, :], m.IDENT[0:72, 0:72]).then_inc(m.s("gains_turned"), 1)


def tables_tensor(pe, m):
    pe.wait_ge(m.consts_in, 16 * m.n_consts)
    for c in range(3):
        w = W_ALL // 3
        ins = mm(pe, m.pb[4 + c][0:HEADS, 0:w], m.RB[:, :], m.HOT[:, c * w:(c + 1) * w], True)
    ins.then_inc(m.s("tables_made"), 1)
    pe.wait_ge(m.s("gains_set"), 1)
    mm(pe, m.pb[7][0:8, 0:W_IDX], m.RBI[:, :], m.HOTI, True).then_inc(m.s("tables_made"), 1)


def sliding(table, start, step, dims):
    size = table.shape[1] * table.shape[2]
    return bass.AP(table.tensor, start, [[size - step * DH, 2], [-step, DH]] + dims)


def tables_scalar(act, m):
    act.wait_ge(m.s("tables_made"), 2)
    w = W_ALL // 3
    for c in range(3):
        act.activation(m.TAB16[:, c * w:(c + 1) * w], m.pb[4 + c][0:HEADS, 0:w], ACT.Copy)\
            .then_inc(m.s("tables_copied"), 1)
    act.activation(m.TAB8, m.pb[7][0:8, 0:W_IDX], ACT.Copy).then_inc(m.s("tables_copied"), 1)


def tables_gpsimd(pool, m):
    pool.wait_ge(m.s("tables_copied"), 4)
    for copy in range(2):
        pool.dma_start(m.TD[copy], m.TAB16).then_inc(m.s("tables_stored"), 16)
        pool.dma_start(m.TDI[copy], m.TAB8).then_inc(m.s("tables_stored"), 16)


def bias_a_gpsimd(pool, m):
    pool.wait_ge(m.s("tables_stored"), 64)
    for h in range(HEADS):
        pool.dma_start(m.BIAS[:, h, :], sliding(m.TD, h * W_ALL + O_NAT + 127, 1, [[1, S]]))\
            .then_inc(m.s("bias_a_in"), 16)



def project_turned(pe, m, n, bank, tiles, src, norm=None):
    for half in range(2):
        if norm is not None:
            wait_rows(pe, m, norm, half)
        pe.wait_ge(m.lo_done, n + half + 1)
        sl = slot(n + half)
        for i, sel in enumerate(tiles):
            for k in range(4):
                kt = 4 * half + k
                wh, wl = sel(m.WH[:, sl, :], k), sel(m.WL[:, sl, :], k)
                ins = mm3(pe, m.pb[bank + i // 2][:, (i % 2) * S:(i % 2 + 1) * S], wh, wl,
                          src[0][:, kt, :], src[1][:, kt, :], kt == 0 and i % 2 == 0)
        ins.then_inc(m.unit_used, 1)


def cols(c):
    return lambda w, k: w[:, k * 512 + c:k * 512 + c + P]


def head_pair(r):
    return lambda w, k: w[:, r * 512 + k * P:r * 512 + (k + 1) * P]


def project_a_sync(sp, m):
    w = m.i["a_w_in"][0].rearrange("(k p) n -> p k n", p=P)
    n = first_unit("a_in")
    for c in range(5):
        for half in range(2):
            load_unit(sp, m, n, [(m.RAW[:, slot(n), :].rearrange("p (k c) -> p k c", k=4),
                                  w[:, 4 * half:4 * half + 4, c * 512:(c + 1) * 512])])
            n += 1
    load_unit(sp, m, n, [(m.RAW[:, slot(n), 0:KT * 48].rearrange("p (k c) -> p k c", k=KT),
                          w[:, :, 2560:2608])])


def project_a_tensor(pe, m):
    n = first_unit("a_in")
    done = m.s("a_projected")
    src = (m.HTH, m.HTL)
    for c in range(5):
        bank = 2 * (c % 2)
        if c == 2:
            tables_tensor(pe, m)
        if c >= 2:
            pe.wait_ge(m.s("a_left_out"), c - 1)
            pe.wait_ge(m.s("a_right_out"), c - 1)
        if c < 2:
            tiles = [head_pair(r) for r in range(4)]
        elif c == 2:
            tiles = [cols(j * P) for j in range(4)]
        else:
            tiles = [cols(j * P) for j in range(2)]
        if c < 3:
            project_turned(pe, m, n, bank, tiles, src, 0 if c == 0 else None)
        else:
            for half in range(2):
                pe.wait_ge(m.lo_done, n + half + 1)
                sl = slot(n + half)
                for k in range(4):
                    kt = 4 * half + k
                    for i, sel in enumerate(tiles):
                        mm3(pe, m.pb[bank][:, i * S:(i + 1) * S], sel(m.WH[:, sl, :], k), sel(m.WL[:, sl, :], k),
                            m.HTH[:, kt, :], m.HTL[:, kt, :], kt == 0 and i == 0)
                    for t in range(TT):
                        tok = slice(t * P, (t + 1) * P)
                        ins = mm3(pe, m.pb[bank + 1][:, t * S:(t + 1) * S], m.HTH[:, kt, tok],
                                  m.HTL[:, kt, tok], m.WH[:, sl, k * 512 + S:(k + 1) * 512],
                                  m.WL[:, sl, k * 512 + S:(k + 1) * 512], kt == 0 and t == 0)
                ins.then_inc(m.unit_used, 1)
        n += 2
    pe.wait_ge(m.lo_done, n + 1)
    pe.wait_ge(m.s("tables_copied"), 4)
    for kt in range(KT):
        for t in range(TT):
            tok = slice(t * P, (t + 1) * P)
            ins = mm3(pe, m.pb[4][:, t * 48:(t + 1) * 48], m.HTH[:, kt, tok], m.HTL[:, kt, tok],
                      m.WH[:, slot(n), kt * 48:(kt + 1) * 48], m.WL[:, slot(n), kt * 48:(kt + 1) * 48],
                      kt == 0 and t == 0)
    ins.then_inc(m.unit_used, 1)


def project_a_scalar(act, m):
    n = first_unit("a_in")
    evac = m.s("a_left_out")

    def block_done(c):
        act.wait_ge(m.unit_used, n + 2 * c + 2)

    split_hi(act, m, n + 2)
    nxt = n + 3
    for c in range(5):
        for _ in range(2):
            if nxt < n + 11:
                split_hi(act, m, nxt)
                nxt += 1
        if c in (1, 2):
            dst, src = ((m.A.W1K, m.i["a_w1_k"]), (m.A.W1V, m.i["a_w1_v"]))[c - 1]
            act.dma_start(dst, src[0].rearrange("(u p) n -> p u n", p=P)).then_inc(m.s("w1_in"), 16)
        block_done(c)
        b = 2 * (c % 2)
        if c == 3:
            tables_scalar(act, m)
        if c < 2:
            act.activation(m.A.QT[:, c, 0:2, :], m.pb[b][:, :].rearrange("p (r t) -> p r t", r=2), ACT.Copy,
                           scale=0.125).then_inc(evac, 1)
        elif c == 2:
            copy_shifted(act, m, m.A.KC2, m.pb[b], True).then_inc(evac, 1)
        elif c == 3:
            act.activation(m.A.KST, m.pb[b][:, :].rearrange("p (g t) -> p g t", g=2), ACT.Copy).then_inc(evac, 1)
        else:
            act.activation(m.A.KWT, m.pb[b][:, :].rearrange("p (g t) -> p g t", g=2), ACT.Copy).then_inc(evac, 1)
    act.wait_ge(m.s("gate_in"), 1)
    act.activation(m.A.GATE, m.A.GATE, ACT.Tanh, scale=0.5).then_inc(m.s("gate_tanh"), 1)


def copy_shifted(eng, m, dst, bank, on_act):
    src = bank[:, :].rearrange("p (g t) -> p g t", g=2)
    for par in range(2):
        rows = src[par * DH:(par + 1) * DH]
        for h in range(2):
            out = dst[h * DH:(h + 1) * DH, par::2, 0:S - h]
            if on_act:
                ins = eng.activation(out, rows[:, :, h:S], ACT.Copy)
            else:
                ins = eng.tensor_copy(out, rows[:, :, h:S])
    return ins


def project_a_vector(dve, m):
    n = first_unit("a_in")
    evac = m.s("a_right_out")
    split_lo(dve, m, n + 2)
    nxt = n + 3
    for c in range(5):
        for _ in range(2):
            if nxt < n + 11:
                split_lo(dve, m, nxt)
                nxt += 1
        dve.wait_ge(m.unit_used, n + 2 * c + 2)
        b = 2 * (c % 2) + 1
        half = m.pb[b][:, :].rearrange("p (r t) -> p r t", r=2)
        if c < 2:
            dve.tensor_scalar(m.A.QT[:, c, 2:4, :], half, 0.125, None, ALU.mult).then_inc(evac, 1)
        elif c == 2:
            copy_shifted(dve, m, m.A.VC2, m.pb[b], False).then_inc(evac, 1)
        elif c == 3:
            dve.tensor_copy(m.A.VS, half).then_inc(evac, 1)
        else:
            dve.tensor_copy(m.A.VW, half).then_inc(evac, 1)
    dve.wait_ge(m.unit_used, n + 11)
    for t in range(TT):
        ins = dve.tensor_tensor(m.A.GATE[:, t, :], m.pb[4][:, t * 48:(t + 1) * 48], m.BGATE[:, :], ALU.add)
    ins.then_inc(m.s("gate_in"), 1)
    dve.wait_ge(m.s("gate_tanh"), 1)
    dve.tensor_scalar(m.A.GATE, m.A.GATE, 1.0, 0.5, ALU.add, ALU.mult).then_inc(m.s("gate_ready"), 1)



def compress_gpsimd(pool, m):
    pool.wait_ge(m.s("a_left_out"), 3)
    pool.wait_ge(m.s("a_right_out"), 3)
    for n, (dst, src) in enumerate(((m.A.RK, m.A.KC2), (m.A.RV, m.A.VC2))):
        for g in range(KV):
            blocks = bass.AP(src.tensor, src.offset + g * S, [list(src.ap[0]), [2, 16], [16, NCMP]])
            ins = pool.tensor_tensor(dst[:, :, g, :], blocks,
                                     m.PE[:, n, :].unsqueeze(2).to_broadcast([P, 16, NCMP]), ALU.add)
        ins.then_inc(m.s("blocks_ready"), 1)
    bias_a_gpsimd(pool, m)
    pool.memset(m.A.KCB, 0.0).then_inc(m.s("padding_zero"), 1)
    pool.wait_ge(m.s("hidden_made"), 2)
    pool.memset(m.A.HID, 0.0).then_inc(m.s("padding_zero"), 1)
    pool.memset(m.A.PC, 0.0).then_inc(m.s("padding_zero"), 1)


def compress_tensor(pe, m):
    blocks, made = m.s("blocks_ready"), m.s("hidden_made")
    pe.wait_ge(m.s("w1_in"), 32)
    pe.wait_ge(m.s("gate_in"), 1)

    def hidden(n, first, last):
        w1, r = ((m.A.W1K, m.A.RK), (m.A.W1V, m.A.RV))[n]
        for u in range(first, last):
            ins = mm(pe, m.pb[4 + n][0:KV * NCMP, 0:S], r[:, u, :, :].rearrange("p g n -> p (g n)"), w1[:, u, :],
                     u == 0, u == 15)
        return ins

    def turn(n):
        pe.wait_ge(m.s(f"gelu{n}_steps"), 6)
        for k in range(2):
            ins = pe.transpose(m.pb[4 + n][:, S + k * 64:S + k * 64 + KV * NCMP],
                               m.A.GX[0:KV * NCMP, k * P:(k + 1) * P], m.IDENT[0:KV * NCMP, 0:KV * NCMP])
        ins.then_inc(m.s("hidden_turned"), 1)

    pe.wait_ge(blocks, 1)
    hidden(0, 0, 16).then_inc(made, 1)
    pe.wait_ge(blocks, 2)
    hidden(1, 0, 8)
    turn(0)
    hidden(1, 8, 16).then_inc(made, 1)
    pe.wait_ge(m.s("k_hidden_copied"), 1)
    for k in range(2):
        ins = mm(pe, m.pb[6][:, 0:60], m.W2[:, 0, k, :], m.A.GH[:, k, 0:60], k == 0, k == 1)
    ins.then_inc(m.s("k_cmp_made"), 1)
    pe.wait_ge(m.s("k_cmp_ready"), 1)
    pe.wait_ge(m.s("a_left_out"), 5)
    pe.wait_ge(m.s("a_right_out"), 5)
    for t in range(TT):
        for T in range(8):
            G, r = T // 4, T % 4
            out = m.pb[t][:, 0:256].rearrange("p (g r n) -> p g r n", g=4, r=4)[:, 2 * G:2 * G + 2, r, :]
            ins = mm(pe, out, m.A.QT[:, G, r, t * P:(t + 1) * P], m.A.KCB[:, G, :, :], T == 0)
        ins.then_inc(m.s("cmp_scored"), 1)
    turn(1)
    pe.wait_ge(m.s("v_hidden_spread"), 1)
    for g in range(KV):
        for k in range(2):
            lhs = m.A.HID[:, k, g, :].rearrange("p r n -> p (r n)")
            ins = mm(pe, m.pb[7][:, g * DH:(g + 1) * DH], lhs, m.W2[:, 1, k, 0:DH], g == 0 and k == 0, k == 1)
    ins.then_inc(m.s("v_cmp_made"), 1)
    pe.wait_ge(m.s("v_cmp_ready"), 1)
    for t in range(TT):
        pe.wait_ge(m.s("cmp_weighted"), t + 1)
        for g in range(KV):
            ins = pe.transpose(m.pb[6 + t][:, g * P:(g + 1) * P],
                               m.A.PC[:, t, g, :, :].rearrange("p r n -> p (r n)"), m.IDENT[:, :])
        ins.then_inc(m.s("cmp_turned"), 1)


def gelu_vector(dve, m, tag, x, y, src, out):
    d = m.s(f"{tag}_steps")
    if src is not None:
        dve.tensor_copy(x, src).then_inc(d, 1)
    dve.wait_ge(d, 1)
    dve.tensor_tensor(y, x, x, ALU.mult).then_inc(d, 1)
    dve.wait_ge(d, 2)
    dve.tensor_scalar(y, y, 0.044715, 1.0, ALU.mult, ALU.add).then_inc(d, 1)
    dve.wait_ge(d, 3)
    dve.tensor_tensor(y, y, x, ALU.mult).then_inc(d, 1)
    dve.wait_ge(m.s(f"{tag}_tanh"), 1)
    dve.tensor_scalar(y, y, 1.0, 0.5, ALU.add, ALU.mult).then_inc(d, 1)
    dve.wait_ge(d, 5)
    return dve.tensor_tensor(out, y, x, ALU.mult).then_inc(d, 1)


def gelu_scalar(act, m, tag, y):
    act.wait_ge(m.s(f"{tag}_steps"), 4)
    act.activation(y, y, ACT.Tanh, scale=math.sqrt(2 / math.pi)).then_inc(m.s(f"{tag}_tanh"), 1)


def compress_scalar(act, m):
    gelu_rows = m.A.GY[0:KV * NCMP]
    gelu_scalar(act, m, "gelu0", gelu_rows)
    act.wait_ge(m.s("k_cmp_made"), 1)
    act.wait_ge(m.s("padding_zero"), 1)
    src = m.pb[6][:, 0:60].rearrange("p (g n) -> p g n", g=KV)
    for par in range(2):
        rows = slice(par * DH, (par + 1) * DH)
        ins = act.activation(m.A.KCB[rows, :, par, 0:NCMP], src[rows, par::2, :], ACT.Copy)
    ins.then_inc(m.s("k_cmp_ready"), 1)
    gelu_scalar(act, m, "gelu1", gelu_rows)
    act.wait_ge(m.s("v_cmp_made"), 1)
    act.activation(m.A.VCR, m.pb[7][:, 0:4 * DH].rearrange("p (g d) -> p g d", g=KV), ACT.Copy)\
        .then_inc(m.s("v_cmp_ready"), 1)
    for t in range(TT):
        act.wait_ge(m.s("cmp_shifted"), t + 1)
        act.activation(m.A.SC[:, t, :, 0:m.ncmp[t]], m.A.SC[:, t, :, 0:m.ncmp[t]], ACT.Exp)\
            .then_inc(m.s("cmp_exp"), 1)
    for t in range(TT):
        act.wait_ge(m.s("cmp_turned"), t + 1)
        act.activation(m.A.PCT[:, :, t * P:(t + 1) * P],
                       m.pb[6 + t][:, :].rearrange("p (g q) -> p g q", g=KV), ACT.Copy)\
            .then_inc(m.s("cmp_ready"), 1)


def compress_vector(dve, m):
    x, y = m.A.GX[0:KV * NCMP], m.A.GY[0:KV * NCMP]
    for n in range(2):
        dve.wait_ge(m.s("hidden_made"), n + 1)
        gelu_vector(dve, m, f"gelu{n}", x, y, m.pb[4 + n][0:KV * NCMP, 0:S], x)
        dve.wait_ge(m.s("hidden_turned"), n + 1)
        turned = m.pb[4 + n][:, S:S + P].rearrange("p (k c) -> p k c", k=2)[:, :, 0:60]
        if n == 0:
            dve.tensor_copy(m.A.GH[:, :, 0:60], turned).then_inc(m.s("k_hidden_copied"), 1)
    dve.wait_ge(m.s("padding_zero"), 2)
    for k in range(2):
        src = turned[:, k, :].rearrange("p (g n) -> p g n", g=KV)
        ins = dve.tensor_copy(m.A.HID[:, k, :, :, 0:NCMP], src.unsqueeze(2).to_broadcast([P, KV, 4, NCMP]))
    ins.then_inc(m.s("v_hidden_spread"), 1)
    d = m.s("cmp_steps")
    dve.wait_ge(m.s("bias_a_in"), 16 * HEADS)
    dve.wait_ge(m.s("gate_ready"), 1)
    n = 0
    for t in range(TT):
        w = m.ncmp[t]
        first = 31 if t == 1 else 159
        sc = m.A.SC[:, t, :, 0:w]
        dve.wait_ge(m.s("cmp_scored"), t + 1)
        for half in range(2):
            hs = slice(8 * half, 8 * half + 8)
            dve.tensor_tensor(m.A.SC[:, t, hs, 0:w], m.pb[t][:, 0:256]
                              .rearrange("p (h n) -> p h n", n=16)[:, hs, 0:w],
                              m.BIAS[:, hs, first:first + 16 * (w - 1) + 1:16], ALU.add).then_inc(d, 1)
        dve.wait_ge(d, n + 2)
        dve.tensor_reduce(m.A.CM[:, t, :], sc, AX_X, ALU.max).then_inc(d, 1)
        dve.wait_ge(d, n + 3)
        dve.tensor_scalar(m.A.CM[:, t, :], m.A.CM[:, t, :], -1e29, None, ALU.max).then_inc(d, 1)
        dve.wait_ge(d, n + 4)
        dve.tensor_tensor(sc, sc, m.A.CM[:, t, :].unsqueeze(2).to_broadcast([P, HEADS, w]), ALU.subtract)\
            .then_inc(m.s("cmp_shifted"), 1)
        dve.wait_ge(m.s("cmp_exp"), t + 1)
        dve.tensor_reduce(m.A.CD[:, t, :], sc, AX_X, ALU.add).then_inc(d, 1)
        dve.wait_ge(d, n + 5)
        dve.tensor_scalar(m.A.CD[:, t, :], m.A.CD[:, t, :], 1e-30, None, ALU.max).then_inc(d, 1)
        dve.wait_ge(d, n + 6)
        dve.reciprocal(m.A.CM[:, t, :], m.A.CD[:, t, :]).then_inc(d, 1)
        dve.wait_ge(d, n + 7)
        dve.tensor_tensor(m.A.CD[:, t, :], m.A.CM[:, t, :],
                          m.A.GATE[:, t, :].rearrange("p (h b) -> p h b", b=3)[:, :, 0], ALU.mult).then_inc(d, 1)
        dve.wait_ge(d, n + 8)
        dve.wait_ge(m.s("padding_zero"), 3)
        dve.tensor_tensor(m.A.PC[:, t, :, :, 0:w].rearrange("p g r n -> p (g r) n"), sc,
                          m.A.CD[:, t, :].unsqueeze(2).to_broadcast([P, HEADS, w]), ALU.mult)\
            .then_inc(m.s("cmp_weighted"), 1)
        n += 8



def inst_a(i):
    T, par, br = i // 4, (i // 2) % 2, i % 2
    G, r = T // 4, T % 4
    return T, G, r, par, br, 4 * (2 * G + par) + r


NA = 32
RINGP = 5
TURN_LAG, SUM_LAG = 3, 4


def attend_a_tensor(pe, m):
    sc, tr, pv = m.s("a_scored"), m.s("a_turned"), m.s("a_summed")
    pe.wait_ge(m.s("cmp_ready"), TT)
    for j in range(NA + SUM_LAG):
        if j < NA:
            T, G, r, par, br, h = inst_a(j)
            rows = slice(par * DH, (par + 1) * DH)
            kt = (m.A.KST, m.A.KWT)[br][rows, G, :]
            if j >= 3:
                pe.wait_ge(m.s("a_biased"), 2 * (j - 2))
            elif j == 0:
                pe.wait_ge(m.s("cmp_shifted"), TT)
            q = m.A.QT[rows, G, r, :]
            mm(pe, m.pb[j % 3][:, 0:S], q[:, P:S], kt, True)
            mm(pe, m.pb[j % 3][:, S:S + P], q[:, 0:P], kt[:, 0:P], False).then_inc(sc, 1)
        if TURN_LAG <= j < NA + TURN_LAG:
            i = j - TURN_LAG
            pe.wait_ge(m.s("a_weighted"), 2 * (i + 1))
            if i >= 2:
                pe.wait_ge(m.s("a_turned_copied"), i - 1)
            w = m.A.PB[:, i % RINGP, :]
            out = m.pb[3 + i % 2]
            pe.transpose(out[:, 0:P], w[:, S:S + P], m.IDENT[:, :])
            pe.transpose(out[:, P:2 * P], w[:, 0:P], m.IDENT[:, :])
            pe.transpose(out[:, 2 * P:3 * P], w[:, P:S], m.IDENT[:, :]).then_inc(tr, 1)
        if j >= SUM_LAG:
            i = j - SUM_LAG
            T, G, r, par, br, h = inst_a(i)
            out = m.pb[5 + T % 2][par * DH:(par + 1) * DH, :]
            g = 2 * G + par
            if br == 0:
                if par == 0 and T >= 2:
                    pe.wait_ge(m.s("a_out_lo"), T - 1)
                rr = slice(32 * r, 32 * r + 32)
                pe.matmul(out[:, 0:S], m.A.VCR[rr, g, :], m.A.PCT[rr, g, :], start=True, stop=False,
                          skip_group_check=True, tile_position=(32 * r, par * DH))
            pe.wait_ge(m.s("a_turned_copied"), i + 1)
            v = (m.A.VS, m.A.VW)[br]
            pt = m.A.PT[:, i % 2, :]
            mm(pe, out[:, 0:S], v[:, 0, g * DH:(g + 1) * DH], pt[:, 0:S], False, False)
            ins = mm(pe, out[:, P:S], v[:, 1, g * DH:(g + 1) * DH], pt[:, S:S + P], False, br == 1)
            ins.then_inc(pv, 1)


def attend_a_vector(dve, m):
    neg, d = m.s("a_biased"), m.s("a_factor")
    for j in range(NA + 2):
        if j < NA:
            T, G, r, par, br, h = inst_a(j)
            dve.wait_ge(m.s("a_scored"), j + 1)
            if j >= RINGP:
                dve.wait_ge(m.s("a_turned"), j - RINGP + 1)
            w = m.A.PB[:, j % RINGP, :]
            for q, (a, b, c) in enumerate(((0, S, 0), (S, S + P, P))):
                dve.tensor_tensor_reduce(out=w[:, a:b], in0=m.pb[j % 3][:, a:b], in1=m.BIAS[:, h, c:c + b - a],
                                         scale=-1.0, scalar=3e38, op0=ALU.add, op1=ALU.min,
                                         accum_out=m.A.NM[:, j, q:q + 1]).then_inc(neg, 1)
        if 1 <= j < NA + 1:
            i = j - 1
            T, G, r, par, br, h = inst_a(i)
            dve.wait_ge(m.s("a_exp"), 2 * (i + 1))
            dve.reciprocal(m.A.RD[:, i, :], m.A.RS[:, i, :]).then_inc(d, 1)
            dve.wait_ge(d, 2 * i + 1)
            g = m.A.GATE[:, :, 3 * h + 1 + br]
            for q in range(2):
                ins = dve.tensor_tensor(m.A.RD[:, i, q:q + 1], m.A.RD[:, i, q:q + 1], g[:, 1 - q:2 - q], ALU.mult)
            ins.then_inc(d, 1)
            dve.wait_ge(d, 2 * i + 2)
            for q, (a, b) in enumerate(((0, S), (S, S + P))):
                w = m.A.PB[:, i % RINGP, a:b]
                dve.tensor_scalar(w, w, m.A.RD[:, i, q:q + 1], None, ALU.mult).then_inc(m.s("a_weighted"), 1)
        if j >= 9 and (j - 9) % 4 == 0:
            T = (j - 9) // 4
            out_lo(dve, m, "a", T, T, m.pb[5 + T % 2][:, 0:S])
    for T in range((NA + 2 - 10) // 4 + 1, 8):
        out_lo(dve, m, "a", T, T, m.pb[5 + T % 2][:, 0:S])


def out_lo(dve, m, x, T, tile, bank_view):
    dve.wait_ge(m.s(f"{x}_out_hi"), T + 1)
    dve.tensor_tensor(out_view(m.OTL[:, tile, :], bank_view), bank_view,
                      out_view(m.OTH[:, tile, :], bank_view).bitcast(F32), ALU.subtract)\
        .then_inc(m.s(f"{x}_out_lo"), 1)


def out_view(row, like):
    return row if len(like.shape) == 2 else row.rearrange("p (i a) -> p i a", a=2)


def attend_a_scalar(act, m):
    def out_hi(T):
        act.wait_ge(m.s("a_summed"), 4 * (T + 1))
        act.activation(m.OTH[:, T, :], m.pb[5 + T % 2][:, 0:S], ACT.Copy).then_inc(m.s("a_out_hi"), 1)

    for j in range(NA + SUM_LAG):
        if j < NA:
            for q, (a, b) in enumerate(((0, S), (S, S + P))):
                act.wait_ge(m.s("a_biased"), 2 * j + q + 1)
                w = m.A.PB[:, j % RINGP, a:b]
                act.activation(w, w, ACT.Exp, bias=m.A.NM[:, j, q:q + 1], scale=-1.0,
                               accum_out=m.A.RS[:, j, q:q + 1]).then_inc(m.s("a_exp"), 1)
        if TURN_LAG <= j < NA + TURN_LAG:
            i = j - TURN_LAG
            act.wait_ge(m.s("a_turned"), i + 1)
            if i >= 2:
                act.wait_ge(m.s("a_summed"), i - 1)
            act.activation(m.A.PT[:, i % 2, 0:3 * P], m.pb[3 + i % 2][:, 0:3 * P], ACT.Copy)\
                .then_inc(m.s("a_turned_copied"), 1)
        if j >= 8 and (j - 8) % 4 == 0:
            out_hi((j - 8) // 4)
    out_hi(7)



def out_sync(sp, m, stage, w, first=0, last=4):
    n = first_unit(stage)
    rows = w.rearrange("(g a r d) n -> g a d r n", g=2, a=2, r=4)
    for c in range(2):
        for G in range(2):
            raw = m.RAW[:, slot(n), :].rearrange("p (r c) -> p r c", r=4)
            if first <= n - first_unit(stage) < last:
                load_unit(sp, m, n, [(raw[a * DH:(a + 1) * DH], rows[G, a, :, :, c * 512:(c + 1) * 512])
                                     for a in range(2)])
            n += 1


def out_tensor(pe, m, stage, src, ready):
    n = first_unit(stage)
    pe.wait_ge(*ready)
    for c in range(2):
        for G in range(2):
            pe.wait_ge(m.lo_done, n + 1)
            for t in range(TT):
                tok = slice(t * P, (t + 1) * P)
                for r in range(4):
                    k = 4 * G + r
                    ins = mm3(pe, m.pb[DOWN_BANK + 2 * t + c][:, :], src[0][:, k, tok], src[1][:, k, tok],
                              m.WH[:, slot(n), r * 512:(r + 1) * 512],
                              m.WL[:, slot(n), r * 512:(r + 1) * 512], k == 0)
                if t == 0 and c == 1 and G == 1:
                    ins.then_inc(m.s("first_tile_done"), 1)
            ins.then_inc(m.unit_used, 1)
            n += 1



def by_parity(row):
    return row.rearrange("p (i a) -> p a i", a=2)


def project_b_sync(sp, m):
    n = first_unit("b_in")
    kv = m.i["kv_w"].rearrange("(k p) n -> p k n", p=P)
    wq = m.i["b_w_q"][0].rearrange("(k p) n -> p k n", p=P)
    for w, c in [(kv, c) for c in range(3)] + [(wq, c) for c in range(6)]:
        for half in range(2):
            load_unit(sp, m, n, [(m.RAW[:, slot(n), :].rearrange("p (k c) -> p k c", k=4),
                                  w[:, 4 * half:4 * half + 4, c * 512:(c + 1) * 512])])
            n += 1


def project_kv_tensor(pe, m, n, bank, lhs_v, norm=None):
    for half in range(2):
        if norm is not None:
            wait_rows(pe, m, norm, half)
        pe.wait_ge(m.lo_done, n + half + 1)
        sl = slot(n + half)
        for k in range(4):
            kt = 4 * half + k
            for i in range(2):
                at = slice(k * 512 + i * P, k * 512 + (i + 1) * P)
                mm3(pe, m.pb[bank][:, i * S:(i + 1) * S], m.WH[:, sl, at], m.WL[:, sl, at],
                    m.HTH[:, kt, :], m.HTL[:, kt, :], kt == 0 and i == 0)
            at = slice(k * 512 + S, (k + 1) * 512)
            for t in range(TT):
                ins = mm3(pe, m.pb[bank + 1][:, t * S:(t + 1) * S], lhs_v(m.HTH[:, kt, :], t),
                          lhs_v(m.HTL[:, kt, :], t), m.WH[:, sl, at], m.WL[:, sl, at], kt == 0 and t == 0)
        ins.then_inc(m.unit_used, 1)


def rows_natural(row, t):
    return row[:, t * P:(t + 1) * P]


def rows_by_parity(row, t):
    return row[:, t::2]


def project_b_tensor(pe, m):
    n = first_unit("b_in")
    for c in range(9):
        bank = 2 * (c % 2)
        if c >= 2:
            pe.wait_ge(m.s("b_left_out"), c - 1)
            pe.wait_ge(m.s("b_right_out"), c - 1)
        if c < 3:
            project_kv_tensor(pe, m, n, bank, rows_by_parity if c else rows_natural, 2 if c == 0 else None)
        else:
            project_turned(pe, m, n, bank, [head_pair(r) for r in range(4)], (m.OTH, m.OTL))
        n += 2


def project_b_scalar(act, m):
    n = first_unit("b_in")
    evac = m.s("b_left_out")
    split_hi(act, m, n + 2)
    nxt = n + 3
    for c in range(9):
        for _ in range(2):
            if nxt < n + 18:
                split_hi(act, m, nxt)
                nxt += 1
        act.wait_ge(m.unit_used, n + 2 * c + 2)
        bank = m.pb[2 * (c % 2)]
        for i in range(2):
            src = bank[:, i * S:(i + 1) * S]
            if c == 0:
                ins = act.activation(m.B.KT[:, c, i, :], src, ACT.Copy)
            elif c < 3:
                ins = act.activation(parities(m.B.KT[:, c, i, :]), by_parity(src), ACT.Copy)
            else:
                ins = act.activation(parities(m.B.QT[:, (c - 3) // 2, (c - 3) % 2, i, :]), by_parity(src),
                                     ACT.Copy, scale=0.125)
        ins.then_inc(evac, 1)


def parities(row):
    return row.rearrange("p (a i) -> p a i", a=2)


def project_b_vector(dve, m):
    n = first_unit("b_in")
    evac = m.s("b_right_out")
    split_lo(dve, m, n + 2)
    nxt = n + 3
    for c in range(9):
        for _ in range(2):
            if nxt < n + 18:
                split_lo(dve, m, nxt)
                nxt += 1
        dve.wait_ge(m.unit_used, n + 2 * c + 2)
        bank = m.pb[2 * (c % 2) + 1]
        if c < 3:
            dve.tensor_copy(m.B.V[:, c, :, :], bank[:, :].rearrange("p (t d) -> p t d", t=TT)).then_inc(evac, 1)
        else:
            for i in range(2):
                ins = dve.tensor_scalar(parities(m.B.QT[:, (c - 3) // 2, (c - 3) % 2, 2 + i, :]),
                                        by_parity(bank[:, i * S:(i + 1) * S]), 0.125, None, ALU.mult)
            ins.then_inc(evac, 1)


NB = 32
RINGB = 4
BW = 768


def bias_b_sync(sp, m, heads):
    sp.wait_ge(m.s("a_biased"), 2 * NA)
    for hh in heads:
        T, par = hh // 2, hh % 2
        h = 4 * (2 * (T // 4) + par) + T % 4
        if hh >= RINGB:
            sp.wait_ge(m.s("b_biased"), 2 * (hh - RINGB) + 2)
        tile = m.BIASB[:, hh % RINGB, :]
        row = h * W_ALL
        for a in range(2):
            sp.dma_start(tile[:, a * 512:a * 512 + S],
                           sliding(m.TD, row + O_G0 + 255 - a, 2, [[1, S]]))\
                .then_inc(m.bias_b_in[hh % RINGB], 16)
        for g, o in ((0, O_G1), (1, O_G2)):
            sp.dma_start(tile[:, S + g * P:S + (g + 1) * P],
                           sliding(m.TD, row + o + 127, 1, [[1, P]]))\
                .then_inc(m.bias_b_in[hh % RINGB], 16)


def attend_b_tensor(pe, m):
    for j in range(NB + SUM_LAG):
        if j < NB:
            T, par, a = j // 4, (j // 2) % 2, j % 2
            G, r = T // 4, T % 4
            rows = slice(par * DH, (par + 1) * DH)
            if j == 0:
                pe.wait_ge(m.s("b_left_out"), 9)
                pe.wait_ge(m.s("b_right_out"), 9)
            if j >= 3:
                pe.wait_ge(m.s("b_biased"), j - 2)
            tok = slice(a * P, (a + 1) * P)
            g0, g1, g2 = ((0, S, S + P), (S, 0, P))[a]
            bank = m.pb[j % 3]
            q = [m.B.QT[rows, g, G, r, tok] for g in range(3)]
            mm(pe, bank[:, g0:g0 + S], q[0], m.B.KT[rows, 0, G, :], True)
            mm(pe, bank[:, g1:g1 + P], q[1], m.B.KT[rows, 1, G, tok], False)
            mm(pe, bank[:, g2:g2 + P], q[2], m.B.KT[rows, 2, G, tok], False).then_inc(m.s("b_scored"), 1)
        if TURN_LAG <= j < NB + TURN_LAG:
            i = j - TURN_LAG
            pe.wait_ge(m.s("b_weighted"), i + 1)
            if i >= 2:
                pe.wait_ge(m.s("b_turned_copied"), i - 1)
            for b in range(4):
                ins = pe.transpose(m.pb[3 + i % 2][:, b * P:(b + 1) * P],
                                   m.B.PB[:, i % RINGP, b * P:(b + 1) * P], m.IDENT[:, :])
            ins.then_inc(m.s("b_turned"), 1)
        if j >= SUM_LAG:
            i = j - SUM_LAG
            T, par, a = i // 4, (i // 2) % 2, i % 2
            g = 2 * (T // 4) + par
            out = m.pb[5 + T % 2][par * DH:(par + 1) * DH, a * P:(a + 1) * P]
            if par == 0 and a == 0 and T >= 2:
                pe.wait_ge(m.s("b_out_lo"), T - 1)
            pe.wait_ge(m.s("b_turned_copied"), i + 1)
            d = slice(g * DH, (g + 1) * DH)
            v = [m.B.V[:, 0, 0, d], m.B.V[:, 0, 1, d], m.B.V[:, 1, a, d], m.B.V[:, 2, a, d]]
            if a == 1:
                v = v[2:] + v[:2]
            for b in range(4):
                ins = mm(pe, out, v[b], m.B.PT[:, i % 2, b * P:(b + 1) * P], a == 0 and b == 0, b == 3)
            ins.then_inc(m.s("b_summed"), 1)


def attend_b_vector(dve, m):
    def lo(T):
        out_lo(dve, m, "b", T, T, m.pb[5 + T % 2][:, 0:S].rearrange("p (a i) -> p i a", a=2))

    for j in range(NB + 2):
        if j < NB:
            a, hh = j % 2, j // 2
            dve.wait_ge(m.bias_b_in[hh % RINGB], 64 * (hh // RINGB + 1))
            dve.wait_ge(m.s("b_scored"), j + 1)
            if j >= RINGP:
                dve.wait_ge(m.s("b_turned"), j - RINGP + 1)
            dve.tensor_tensor_reduce(out=m.B.PB[:, j % RINGP, :], in0=m.pb[j % 3][:, :],
                                     in1=m.BIASB[:, hh % RINGB, a * S:a * S + 512], scale=-1.0, scalar=3e38,
                                     op0=ALU.add, op1=ALU.min, accum_out=m.B.NM[:, j:j + 1])\
                .then_inc(m.s("b_biased"), 1)
        if 1 <= j < NB + 1:
            i = j - 1
            dve.wait_ge(m.s("b_exp"), i + 1)
            dve.reciprocal(m.B.RD[:, i:i + 1], m.B.RS[:, i:i + 1]).then_inc(m.s("b_factor"), 1)
            dve.wait_ge(m.s("b_factor"), i + 1)
            w = m.B.PB[:, i % RINGP, :]
            dve.tensor_scalar(w, w, m.B.RD[:, i:i + 1], None, ALU.mult).then_inc(m.s("b_weighted"), 1)
        if j >= 9 and (j - 9) % 4 == 0:
            lo((j - 9) // 4)
    lo(7)


def attend_b_scalar(act, m):
    def hi(T):
        act.wait_ge(m.s("b_summed"), 4 * (T + 1))
        bank = m.pb[5 + T % 2][:, 0:S].rearrange("p (a i) -> p i a", a=2)
        act.activation(out_view(m.OTH[:, T, :], bank), bank, ACT.Copy).then_inc(m.s("b_out_hi"), 1)

    for j in range(NB + SUM_LAG):
        if j < NB:
            act.wait_ge(m.s("b_biased"), j + 1)
            w = m.B.PB[:, j % RINGP, :]
            act.activation(w, w, ACT.Exp, bias=m.B.NM[:, j:j + 1], scale=-1.0,
                           accum_out=m.B.RS[:, j:j + 1]).then_inc(m.s("b_exp"), 1)
        if TURN_LAG <= j < NB + TURN_LAG:
            i = j - TURN_LAG
            act.wait_ge(m.s("b_turned"), i + 1)
            if i >= 2:
                act.wait_ge(m.s("b_summed"), i - 1)
            act.activation(m.B.PT[:, i % 2, :], m.pb[3 + i % 2][:, :], ACT.Copy)\
                .then_inc(m.s("b_turned_copied"), 1)
        if j >= 8 and (j - 8) % 4 == 0:
            hi((j - 8) // 4)
    hi(7)



def row_norm_scalar(act, m, k, ready):
    sem, value, per_tile = ready
    for t in range(TT):
        act.wait_ge(sem, value + per_tile * t)
        act.activation(m.HN[:, t, :], m.XR[:, t, :], ACT.Square,
                       accum_out=m.SS[:, t:t + 1]).then_inc(m.s("row_norm_squared"), 1)


def row_norm_gpsimd(pool, m, k, ready, gain):
    pool.wait_ge(*ready)
    pool.dma_start(m.GB, bass.AP(gain.tensor, 0, [[0, P], [1, D]])).then_inc(m.s("row_norm_gain_in"), 16)
    pool.wait_ge(m.s("row_norm_mean"), k + 1)
    pool.tensor_tensor(m.RS[:, 0:TT], m.MS[:, 0:TT], m.NEGHALF[:, 0:TT], ALU.pow)\
        .then_inc(m.s("row_norm_rsqrt"), 1)


def row_norm_vector(dve, m, k, done):
    dve.wait_ge(m.s("row_norm_squared"), TT * (k + 1))
    dve.tensor_scalar(m.MS[:, 0:TT], m.SS[:, 0:TT], 1.0 / D, EPS, ALU.mult, ALU.add)\
        .then_inc(m.s("row_norm_mean"), 1)
    dve.wait_ge(m.s("row_norm_rsqrt"), k + 1)
    dve.wait_ge(m.s("row_norm_gain_in"), 16 * (k + 1))
    for t in range(TT):
        dve.scalar_tensor_tensor(out=m.XR[:, t, :], in0=m.XR[:, t, :], scalar=m.RS[:, t:t + 1], in1=m.GB,
                                 op0=ALU.mult, op1=ALU.mult).then_inc(done, 1)



HEAD_NORMS = {"mk": 0, "q0": 1, "q1": 2, "k": 3, "mq": 4}


def head_norm_scalar(act, m, tag, raw, sq):
    act.activation(sq, raw, ACT.Square).then_inc(m.s("head_squared"), 1)


def head_norm_tensor(pe, m, tag, bank, sq):
    pe.wait_ge(m.s("head_squared"), HEAD_NORMS[tag] + 1)
    mm(pe, bank, m.ONES64[:, :], sq, True).then_inc(m.s("head_summed"), 1)


def head_norm_vector_mean(dve, m, tag, bank, ms):
    dve.wait_ge(m.s("head_summed"), HEAD_NORMS[tag] + 1)
    dve.tensor_scalar(ms, bank, 1.0 / DH, EPS, ALU.mult, ALU.add).then_inc(m.s("head_mean"), 1)


def head_norm_root(act, m, tag, ms):
    act.wait_ge(m.s("head_mean"), HEAD_NORMS[tag] + 1)
    act.activation(ms, ms, ACT.Sqrt).then_inc(m.s("head_root"), 1)


def head_norm_vector_scale(dve, m, tag, out, raw, gain, ms):
    dve.wait_ge(m.s("head_root"), HEAD_NORMS[tag] + 1)
    dve.reciprocal(ms, ms).then_inc(m.s("head_inverse"), 1)
    dve.wait_ge(m.s("head_inverse"), HEAD_NORMS[tag] + 1)
    dve.scalar_tensor_tensor(out=out, in0=raw, scalar=gain, in1=ms, op0=ALU.mult, op1=ALU.mult)\
        .then_inc(m.s("head_done"), 1)



def memory_sync(sp, m):
    n = first_unit("mem_kv")
    w = m.i["w_mem_kv_2"][0].rearrange("(k p) n -> p k n", p=P)
    for half in range(2):
        load_unit(sp, m, n, [(m.RAW[:, slot(n), :].rearrange("p (k c) -> p k c", k=4),
                              w[:, 4 * half:4 * half + 4, :])])
        n += 1


def memory_tensor(pe, m):
    n = first_unit("mem_kv")
    project_kv_tensor(pe, m, n, 0, rows_natural, 5)


def memory_scalar(act, m):
    n = first_unit("mem_kv")
    act.wait_ge(m.unit_used, n + 2)
    act.activation(m.C.MKR, m.pb[0][:, :], ACT.Copy).then_inc(m.s("mk_raw"), 1)
    act.wait_ge(m.s("mk_raw"), 1)
    head_norm_scalar(act, m, "mk", m.C.MKR, m.C.SQMK)


def memory_vector(dve, m):
    n = first_unit("mem_kv")
    dve.wait_ge(m.unit_used, n + 2)
    dve.tensor_copy(m.C.MV, m.pb[1][:, :].rearrange("p (t d) -> p t d", t=TT)).then_inc(m.s("mv_ready"), 1)



C_BLOCKS = (0, 512, 964)


def project_c_sync(sp, m):
    n = first_unit("c_in")
    w = m.i["w_in_2"][0].rearrange("(k p) n -> p k n", p=P)
    for c in C_BLOCKS:
        for half in range(2):
            load_unit(sp, m, n, [(m.RAW[:, slot(n), :].rearrange("p (k c) -> p k c", k=4),
                                  w[:, 4 * half:4 * half + 4, c:c + 512])])
            n += 1


def project_c_tensor(pe, m):
    n = first_unit("c_in")
    src = (m.HTH, m.HTL)
    head_norm_tensor(pe, m, "mk", m.pb[7][:, :], m.C.SQMK)
    tiles = [cols(j * P) for j in range(4)]
    project_turned(pe, m, n, 0, tiles, src, 6)
    for half in range(2):
        pe.wait_ge(m.lo_done, n + 2 + half + 1)
        sl = slot(n + 2 + half)
        for k in range(4):
            kt = 4 * half + k
            for t in range(TT):
                tok = slice(t * P, (t + 1) * P)
                for at, w, o in ((DH, DH, 0), (448, 4, DH)):
                    a = slice(k * 512 + at, k * 512 + at + w)
                    mm3(pe, m.pb[4][:, t * 68 + o:t * 68 + o + w], m.HTH[:, kt, tok], m.HTL[:, kt, tok],
                        m.WH[:, sl, a], m.WL[:, sl, a], kt == 0 and t == 0 and o == 0)
        for i, sel in enumerate(tiles):
            for k in range(4):
                kt = 4 * half + k
                wh, wl = sel(m.WH[:, sl, :], k), sel(m.WL[:, sl, :], k)
                ins = mm3(pe, m.pb[2 + i // 2][:, (i % 2) * S:(i % 2 + 1) * S], wh, wl,
                          m.HTH[:, kt, :], m.HTL[:, kt, :], kt == 0 and i % 2 == 0)
        ins.then_inc(m.unit_used, 1)
    pe.wait_ge(m.s("c_evacuated"), 2)
    for x in range(2):
        head_norm_tensor(pe, m, f"q{x}", m.pb[5 + x][:, :], m.C.SQ[:, x, :])
    project_turned(pe, m, n + 4, 0, tiles, src)
    pe.wait_ge(m.s("head_mean"), 1)
    head_norm_tensor(pe, m, "k", m.pb[7][:, 0:S], m.C.SQK)
    pe.wait_ge(m.s("c_evacuated_vector"), 2)
    head_norm_tensor(pe, m, "mq", m.pb[4][:, :], m.C.SQM)


def project_c_scalar(act, m):
    n = first_unit("c_in")
    ev = m.s("c_evacuated")
    for j in range(2, 4):
        split_hi(act, m, n + j)
    act.wait_ge(m.unit_used, n + 2)
    head_norm_root(act, m, "mk", m.C.MSMK)
    for x in range(2):
        act.activation(m.C.QR[:, x, :], m.pb[x][:, :], ACT.Copy).then_inc(ev, 1)
    act.wait_ge(ev, 2)
    for x in range(2):
        head_norm_scalar(act, m, f"q{x}", m.C.QR[:, x, :], m.C.SQ[:, x, :])
    for j in range(4, 6):
        split_hi(act, m, n + j)
    act.wait_ge(m.unit_used, n + 4)
    act.activation(m.C.KR[0:DH, :], m.pb[2][0:DH, 0:S], ACT.Copy)
    act.activation(m.C.KR[DH:P, :], m.pb[2][0:DH, 0:S], ACT.Copy)
    act.activation(m.C.QI[:, 0, :], m.pb[2][:, S:2 * S], ACT.Copy)
    act.activation(m.C.QI[:, 1, :], m.pb[3][:, 0:S], ACT.Copy)
    act.activation(m.C.KI[0:DH, :], m.pb[3][0:DH, S:2 * S], ACT.Copy)
    act.activation(m.C.KI[DH:P, :], m.pb[3][0:DH, S:2 * S], ACT.Copy).then_inc(ev, 1)
    act.wait_ge(ev, 3)
    head_norm_scalar(act, m, "k", m.C.KR, m.C.SQK)
    for x in range(2):
        head_norm_root(act, m, f"q{x}", m.C.MS2[:, x, :])
    act.wait_ge(m.unit_used, n + 6)
    act.activation(m.C.QMR, m.pb[1][:, :], ACT.Copy).then_inc(ev, 1)
    act.wait_ge(ev, 4)
    head_norm_scalar(act, m, "mq", m.C.QMR, m.C.SQM)
    for tag, ms in (("k", m.C.MSK), ("mq", m.C.MSM)):
        head_norm_root(act, m, tag, ms)


def project_c_vector(dve, m):
    n = first_unit("c_in")
    ev = m.s("c_evacuated_vector")
    head_norm_vector_mean(dve, m, "mk", m.pb[7][:, :], m.C.MSMK)
    for j in range(2, 6):
        split_lo(dve, m, n + j)
    head_norm_vector_scale(dve, m, "mk", m.C.MKT, m.C.MKR, m.HG[:, 3:4], m.C.MSMK)
    dve.wait_ge(m.unit_used, n + 4)
    rows = m.pb[4][:, 0:136].rearrange("p (t c) -> p t c", t=TT)
    dve.tensor_copy(m.C.VA, rows[:, :, 0:DH]).then_inc(ev, 1)
    dve.tensor_scalar(m.C.WI, rows[:, :, DH:DH + 4], 0.0625, None, ALU.mult).then_inc(ev, 1)
    dve.tensor_scalar(m.C.HGS[:, 0:1], m.HG[:, 0:1], 0.125, None, ALU.mult).then_inc(ev, 1)
    dve.tensor_scalar(m.C.HGS[:, 1:2], m.HG[:, 2:3], 0.125, None, ALU.mult).then_inc(ev, 1)
    dve.wait_ge(ev, 4)
    for x in range(2):
        head_norm_vector_mean(dve, m, f"q{x}", m.pb[5 + x][:, :], m.C.MS2[:, x, :])
    for x in range(2):
        head_norm_vector_scale(dve, m, f"q{x}", m.C.QT[:, x, :], m.C.QR[:, x, :], m.C.HGS[:, 0:1],
                               m.C.MS2[:, x, :])
    dve.wait_ge(m.unit_used, n + 6)
    dve.tensor_copy(m.C.UT, m.pb[0][:, :].rearrange("p (j t) -> p j t", j=2)).then_inc(ev, 1)
    dve.wait_ge(ev, 5)
    head_norm_vector_mean(dve, m, "k", m.pb[7][:, 0:S], m.C.MSK)
    head_norm_vector_mean(dve, m, "mq", m.pb[4][:, :], m.C.MSM)


def head_norms_c_vector(dve, m):
    head_norm_vector_scale(dve, m, "k", m.C.KT, m.C.KR, m.HG[:, 1:2], m.C.MSK)
    head_norm_vector_scale(dve, m, "mq", m.C.QM, m.C.QMR, m.C.HGS[:, 1:2], m.C.MSM)



HALVES = ((0, S, 1, 0), (S, S + P, 0, P))


def index_tensor(pe, m):
    pe.wait_ge(m.s("c_evacuated"), 4)
    pe.wait_ge(m.s("c_evacuated_vector"), 5)
    for h in range(4):
        rows = slice((h % 2) * DH, (h % 2 + 1) * DH)
        q, k = m.C.QI[rows, h // 2, :], m.C.KI[rows, :]
        mm(pe, m.pb[h][:, 0:S], q[:, P:S], k, True)
        mm(pe, m.pb[h][:, S:S + P], q[:, 0:P], k[:, 0:P], False).then_inc(m.s("i_scored"), 1)


def index_scalar(act, m):
    for h in range(4):
        act.wait_ge(m.s("i_scored"), h + 1)
        act.activation(m.C.RL[:, h, :], m.pb[h][:, 0:S + P], ACT.Relu).then_inc(m.s("i_relu"), 1)


def index_scores_vector(dve, m):
    d = m.s("i_steps")
    dve.memset(m.C.IS, 0.0).then_inc(d, 1)
    n = 1
    for h in range(4):
        dve.wait_ge(m.s("i_relu"), h + 1)
        dve.wait_ge(d, n)
        for a, b, t, _ in HALVES:
            dve.scalar_tensor_tensor(out=m.C.IS[:, a:b], in0=m.C.RL[:, h, a:b], scalar=m.C.WI[:, t, h:h + 1],
                                     in1=m.C.IS[:, a:b], op0=ALU.mult, op1=ALU.add).then_inc(d, 1)
        n += 2
    dve.wait_ge(d, n)
    dve.memset(m.C.IS[0:DH, S - DH:S], MASKED).then_inc(d, 1)
    dve.memset(m.C.IS[0:DH, S + DH:S + P], MASKED).then_inc(d, 1)


def index_round_vector(dve, m, r):
    d, n = m.s("i_steps"), 11 + 4 * r
    dve.wait_ge(d, n)
    for x, (a, b, _, _) in enumerate(HALVES):
        dve.max(m.C.TOP[:, x, :], m.C.IS[:, a:b]).then_inc(d, 1)
    dve.wait_ge(d, n + 2)
    for x, (a, b, _, _) in enumerate(HALVES):
        dve.match_replace(m.C.IS[:, a:b], m.C.TOP[:, x, :], m.C.IS[:, a:b], TAKEN).then_inc(d, 1)


def index_choice_vector(dve, m):
    dve.wait_ge(m.s("i_steps"), 11 + 4 * (IDX_TOPK // 8))
    dve.tensor_scalar(m.C.SM, m.C.IS, TAKEN, NEG, ALU.not_equal, ALU.mult).then_inc(m.s("i_chosen"), 1)



NC = 12


def inst_c(i):
    return (False, i, i // 2) if i < 8 else (True, i - 8, 6 + (i - 8) // 2)


def attend_c_gpsimd(pool, m):
    pool.wait_ge(m.s("bias_c_in"), 16 * 8)
    pool.wait_ge(m.s("i_chosen"), 1)
    for j in range(8):
        if j >= 2:
            pool.wait_ge(m.s("c_biased"), 2 * (j - 1))
        for a, b, _, c in HALVES:
            pool.tensor_tensor(m.C.BM[:, j % 2, a:b], m.C.SM[:, a:b], m.BIASC[:, j, c:c + b - a], ALU.add)\
                .then_inc(m.s("c_bias_ready"), 1)


def attend_c_tensor(pe, m):
    pe.wait_ge(m.s("head_done"), 5)
    pe.wait_ge(m.s("mv_ready"), 1)
    pe.wait_ge(m.s("i_relu"), 4)
    pe.wait_ge(m.s("s5g_steps"), 1)
    for j in range(NC + SUM_LAG):
        if j < NC:
            mem, h, tile = inst_c(j)
            if j >= 3:
                pe.wait_ge(m.s("c_biased"), 2 * (j - 2))
            rows = slice((h % 2) * DH, (h % 2 + 1) * DH)
            bank = m.pb[j % 3]
            if mem:
                q = m.C.QM[rows, (h // 2) * S:(h // 2 + 1) * S]
                k = m.C.MKT[rows, (h // 2) * S:(h // 2 + 1) * S]
                mm(pe, bank[:, 0:S], q[:, P:S], k, True)
                ins = mm(pe, bank[:, S:2 * S], q[:, 0:P], k, False)
            else:
                q = m.C.QT[rows, h // 4, (h // 2 % 2) * S:(h // 2 % 2 + 1) * S]
                mm(pe, bank[:, 0:S], q[:, P:S], m.C.KT[rows, :], True)
                ins = mm(pe, bank[:, S:S + P], q[:, 0:P], m.C.KT[rows, 0:P], False)
            ins.then_inc(m.s("c_scored"), 1)
        if TURN_LAG <= j < NC + TURN_LAG:
            i = j - TURN_LAG
            mem = inst_c(i)[0]
            pe.wait_ge(m.s("c_weighted"), 2 * (i + 1))
            if i >= 2:
                pe.wait_ge(m.s("c_turned_copied"), i - 1)
            w = m.C.PB[:, i % RINGP, :]
            order = ((S, 0), (0, P), (S + P, 2 * P), (P, 3 * P)) if mem else ((S, 0), (0, P), (P, 2 * P))
            for a, o in order:
                ins = pe.transpose(m.pb[3 + i % 2][:, o:o + P], w[:, a:a + P], m.IDENT[:, :])
            ins.then_inc(m.s("c_turned"), 1)
        if j >= SUM_LAG:
            i = j - SUM_LAG
            mem, h, tile = inst_c(i)
            T = i // 2
            out = m.pb[5 + T % 2][(h % 2) * DH:(h % 2 + 1) * DH, :]
            if h % 2 == 0 and T >= 2:
                pe.wait_ge(m.s("c_out_lo"), T - 1)
            pe.wait_ge(m.s("c_turned_copied"), i + 1)
            pt = m.C.PT[:, i % 2, :]
            if mem:
                v = m.C.MV[:, :, h * DH:(h + 1) * DH]
                mm(pe, out[:, 0:S], v[:, 0, :], pt[:, 0:S], True, False)
                ins = mm(pe, out[:, 0:S], v[:, 1, :], pt[:, S:2 * S], False)
            else:
                mm(pe, out[:, 0:S], m.C.VA[:, 0, :], pt[:, 0:S], True, False)
                ins = mm(pe, out[:, P:S], m.C.VA[:, 1, :], pt[:, S:S + P], False)
            ins.then_inc(m.s("c_summed"), 1)


def attend_c_vector(dve, m):
    def lo(T):
        out_lo(dve, m, "c", T, inst_c(2 * T)[2], m.pb[5 + T % 2][:, 0:S])

    for j in range(NC + 2):
        if j < NC:
            mem = inst_c(j)[0]
            dve.wait_ge(m.s("c_scored"), j + 1)
            if j >= RINGP:
                dve.wait_ge(m.s("c_turned"), j - RINGP + 1)
            for q, (a, b) in enumerate(((0, S), (S, 2 * S if mem else S + P))):
                if not mem:
                    dve.wait_ge(m.s("c_bias_ready"), 2 * j + q + 1)
                bias = m.C.ZERO[:, 0:b - a] if mem else m.C.BM[:, j % 2, a:b]
                dve.tensor_tensor_reduce(out=m.C.PB[:, j % RINGP, a:b], in0=m.pb[j % 3][:, a:b], in1=bias,
                                         scale=-1.0, scalar=3e38, op0=ALU.add, op1=ALU.min,
                                         accum_out=m.C.NM[:, j, q:q + 1]).then_inc(m.s("c_biased"), 1)
        if 1 <= j < NC + 1:
            i = j - 1
            dve.wait_ge(m.s("c_exp"), 2 * (i + 1))
            dve.reciprocal(m.C.RD[:, i, :], m.C.RS[:, i, :]).then_inc(m.s("c_factor"), 1)
            dve.wait_ge(m.s("c_factor"), i + 1)
            for q, (a, b) in enumerate(((0, S), (S, 2 * S if inst_c(i)[0] else S + P))):
                w = m.C.PB[:, i % RINGP, a:b]
                dve.tensor_scalar(w, w, m.C.RD[:, i, q:q + 1], None, ALU.mult).then_inc(m.s("c_weighted"), 1)
        if j >= 7 and (j - 7) % 2 == 0:
            lo((j - 7) // 2)
    for T in range(4, 6):
        lo(T)


def attend_c_scalar(act, m):
    def hi(T):
        act.wait_ge(m.s("c_summed"), 2 * (T + 1))
        act.activation(m.OTH[:, inst_c(2 * T)[2], :], m.pb[5 + T % 2][:, 0:S], ACT.Copy)\
            .then_inc(m.s("c_out_hi"), 1)

    for j in range(NC + SUM_LAG):
        if j < NC:
            mem = inst_c(j)[0]
            for q, (a, b) in enumerate(((0, S), (S, 2 * S if mem else S + P))):
                act.wait_ge(m.s("c_biased"), 2 * j + q + 1)
                w = m.C.PB[:, j % RINGP, a:b]
                act.activation(w, w, ACT.Exp, bias=m.C.NM[:, j, q:q + 1], scale=-1.0,
                               accum_out=m.C.RS[:, j, q:q + 1]).then_inc(m.s("c_exp"), 1)
        if TURN_LAG <= j < NC + TURN_LAG:
            i = j - TURN_LAG
            w = 4 * P if inst_c(i)[0] else 3 * P
            act.wait_ge(m.s("c_turned"), i + 1)
            if i >= 2:
                act.wait_ge(m.s("c_summed"), i - 1)
            act.activation(m.C.PT[:, i % 2, 0:w], m.pb[3 + i % 2][:, 0:w], ACT.Copy)\
                .then_inc(m.s("c_turned_copied"), 1)
        if j >= 6 and (j - 6) % 2 == 0 and (j - 6) // 2 < 5:
            hi((j - 6) // 2)
    hi(5)



NPAIR = 8
TWO_PI_1 = 6.28125
TWO_PI_2 = float(np.float32(2 * math.pi - TWO_PI_1) - np.float32(np.float32(2 * math.pi - TWO_PI_1) % np.float32(2.0 ** -21)))
TWO_PI_3 = 2 * math.pi - TWO_PI_1 - TWO_PI_2
ROUND = 1.5 * 2.0 ** 23
PI_F32 = 3.1415925


def state_loads_gpsimd(pool, m, ready):
    C, i = m.C, m.i
    pool.wait_ge(*ready)
    per_state = [[1, P], [P, NPAIR]]
    loads = [(C.LR, bass.AP(i["ssm_lambda_re_2"].tensor, 0, per_state)),
             (C.LI, bass.AP(i["ssm_lambda_im_2"].tensor, 0, per_state))]
    loads += [(C.DT[g * DH:(g + 1) * DH, :], bass.AP(i["ssm_log_dt_2"].tensor, g, [[0, DH], [2, NPAIR]]))
              for g in range(2)]
    loads += [(C.BN[:, n], bass.AP(t.tensor, 0, [[16, P], [16 * P, NPAIR], [1, 16]]))
              for n, t in enumerate((i["ssm_b_re_2"], i["ssm_b_im_2"]))]
    loads += [(C.CN[:, n, :, h * DH:(h + 1) * DH], bass.AP(t.tensor, 0, [[DH, P], [DH * P, 2], [1, DH]]))
              for n, t in enumerate((i["ssm_c_re_2"], i["ssm_c_im_2"])) for h in range(2)]
    loads += [(C.DCOL, bass.AP(i["ssm_d_2"].tensor, 0, [[1, P], [P, 2]]))]
    for dst, src in loads:
        pool.dma_start(dst, src).then_inc(m.s("s5_in"), 16)
    pool.wait_ge(m.s("s5_in"), 16 * len(loads))
    for n in range(2):
        for h in range(2):
            w = C.CN[:, n, :, h * DH:(h + 1) * DH]
            ins = pool.tensor_scalar(w, w, m.PAR[:, h:h + 1], (1.0, -1.0)[n], ALU.mult, ALU.mult)
    ins.then_inc(m.s("s5_c_masked"), 1)


def state_params_gpsimd(pool, m):
    C, step = m.C, m.s("s5_steps")
    count = [0]

    def link(ins):
        count[0] += 1
        ins.then_inc(step, 1)
        pool.wait_ge(step, count[0])

    pool.wait_ge(m.s("s5_dt"), 1)
    T = C.T
    link(pool.tensor_tensor(T[:, 0], C.LR, C.DT, ALU.mult))
    link(pool.tensor_tensor(T[:, 1], C.LI, C.DT, ALU.mult))
    link(pool.tensor_scalar(T[:, 2], T[:, 1], 1 / (2 * math.pi), ROUND, ALU.mult, ALU.add))
    link(pool.tensor_scalar(T[:, 2], T[:, 2], ROUND, None, ALU.subtract))
    for part in (TWO_PI_1, TWO_PI_2, TWO_PI_3):
        link(pool.tensor_scalar(T[:, 3], T[:, 2], part, None, ALU.mult))
        link(pool.tensor_tensor(T[:, 1], T[:, 1], T[:, 3], ALU.subtract))
    link(pool.tensor_scalar(T[:, 1], T[:, 1], PI_F32, -PI_F32, ALU.min, ALU.max))
    link(pool.tensor_scalar(T[:, 2], T[:, 1], 0.5, None, ALU.mult))
    pool.memset(T[:, 3], 0.0).then_inc(m.s("s5_angle"), 1)
    pool.wait_ge(m.s("s5_functions"), 3)
    link(pool.tensor_tensor(T[:, 4], T[:, 2], T[:, 2], ALU.mult))
    link(pool.tensor_scalar(C.COS, T[:, 4], -2.0, 1.0, ALU.mult, ALU.add))
    link(pool.tensor_tensor(T[:, 5], C.MAG, C.COS, ALU.mult))
    link(pool.tensor_scalar(T[:, 5], T[:, 5], 1.0, None, ALU.subtract))
    link(pool.tensor_tensor(T[:, 6], C.MAG, C.SIN, ALU.mult))
    link(pool.tensor_tensor(T[:, 7], C.LR, C.LR, ALU.mult))
    link(pool.tensor_tensor(T[:, 8], C.LI, C.LI, ALU.mult))
    link(pool.tensor_tensor(T[:, 7], T[:, 7], T[:, 8], ALU.add))
    link(pool.tensor_tensor(T[:, 7], T[:, 7], m.NEGHALF[:, 2:3].to_broadcast([P, NPAIR]), ALU.pow))
    link(pool.tensor_tensor(T[:, 8], T[:, 5], C.LR, ALU.mult))
    link(pool.tensor_tensor(T[:, 9], T[:, 6], C.LI, ALU.mult))
    link(pool.tensor_tensor(T[:, 8], T[:, 8], T[:, 9], ALU.add))
    link(pool.tensor_tensor(T[:, 8], T[:, 8], T[:, 7], ALU.mult))
    link(pool.tensor_tensor(T[:, 9], T[:, 6], C.LR, ALU.mult))
    link(pool.tensor_tensor(T[:, 10], T[:, 5], C.LI, ALU.mult))
    link(pool.tensor_tensor(T[:, 9], T[:, 9], T[:, 10], ALU.subtract))
    link(pool.tensor_tensor(T[:, 9], T[:, 9], T[:, 7], ALU.mult))
    link(pool.memset(C.BX, 0.0))
    fr, fi = (T[:, n].unsqueeze(2).to_broadcast([P, NPAIR, 16]) for n in (8, 9))
    for n, (f, g, op) in enumerate(((fr, fi, ALU.subtract), (fi, fr, ALU.add))):
        link(pool.tensor_tensor(C.BW[:, 0], C.BN[:, 0], f, ALU.mult))
        link(pool.tensor_tensor(C.BW[:, 1], C.BN[:, 1], g, ALU.mult))
        for h in range(2):
            rows = slice(h * DH, (h + 1) * DH)
            link(pool.tensor_tensor(C.BX[rows, n, :, h * 16:(h + 1) * 16], C.BW[rows, 0], C.BW[rows, 1], op))
    pool.memset(T[:, 3], 0.0).then_inc(m.s("s5_b_ready"), 1)


def state_tables_gpsimd(pool, m):
    C, step, T = m.C, m.s("s5_table_steps"), m.C.T
    count = [0]

    def link(ins):
        count[0] += 1
        ins.then_inc(step, 1)
        pool.wait_ge(step, count[0])

    link(pool.memset(C.EC[:, :, 0:1], 1.0))
    link(pool.memset(C.ES[:, :, 0:1], 0.0))
    link(pool.tensor_copy(T[:, 0], C.COS))
    link(pool.tensor_copy(T[:, 1], C.SIN))
    n = 1
    while n < S:
        wc, ws = (T[:, x].unsqueeze(2).to_broadcast([P, NPAIR, n]) for x in (0, 1))
        c0, s0 = C.EC[:, :, 0:n], C.ES[:, :, 0:n]
        t0, t1 = C.ET[:, 0, :, 0:n], C.ET[:, 1, :, 0:n]
        link(pool.tensor_tensor(t0, c0, wc, ALU.mult))
        link(pool.tensor_tensor(t1, s0, ws, ALU.mult))
        link(pool.tensor_tensor(C.EC[:, :, n:2 * n], t0, t1, ALU.subtract))
        link(pool.tensor_tensor(t0, c0, ws, ALU.mult))
        link(pool.tensor_tensor(t1, s0, wc, ALU.mult))
        link(pool.tensor_tensor(C.ES[:, :, n:2 * n], t0, t1, ALU.add))
        link(pool.tensor_tensor(T[:, 4], T[:, 0], T[:, 0], ALU.mult))
        link(pool.tensor_tensor(T[:, 5], T[:, 1], T[:, 1], ALU.mult))
        link(pool.tensor_tensor(T[:, 1], T[:, 0], T[:, 1], ALU.mult))
        link(pool.tensor_tensor(T[:, 0], T[:, 4], T[:, 5], ALU.subtract))
        link(pool.tensor_scalar(T[:, 1], T[:, 1], 2.0, None, ALU.mult))
        n *= 2
    pool.memset(T[:, 3], 0.0).then_inc(m.s("s5_tables"), 1)


def state_step_scalar(act, m):
    act.wait_ge(m.s("s5_in"), 16 * 11)
    act.activation(m.C.DT, m.C.DT, ACT.Exp).then_inc(m.s("s5_dt"), 1)


def state_functions_scalar(act, m):
    act.wait_ge(m.s("s5_angle"), 1)
    f = m.s("s5_functions")
    act.activation(m.C.MAG, m.C.T[:, 0], ACT.Exp).then_inc(f, 1)
    act.activation(m.C.SIN, m.C.T[:, 1], ACT.Sin).then_inc(f, 1)
    act.activation(m.C.T[:, 2], m.C.T[:, 2], ACT.Sin).then_inc(f, 1)


def state_turn_tensor(pe, m):
    pe.wait_ge(m.s("s5_b_ready"), 1)
    pe.wait_ge(m.s("s5_c_masked"), 1)
    for n in range(2):
        for jj in range(2):
            at = slice((2 * n + jj) * P, (2 * n + jj + 1) * P)
            pe.transpose(m.pb[5][:, at], m.C.BX[:, n, 4 * jj:4 * jj + 4, :].rearrange("p j c -> p (j c)"),
                         m.IDENT[:, :])
            ins = pe.transpose(m.pb[6][:, at], m.C.CN[:, n, jj, :], m.IDENT[:, :])
    ins.then_inc(m.s("s5_turned"), 1)


def state_turn_scalar(act, m):
    act.wait_ge(m.s("s5_turned"), 1)
    act.activation(m.C.BT, m.pb[5][:, :].rearrange("p (n j c) -> p n j c", n=2, j=2), ACT.Copy)\
        .then_inc(m.s("s5_turned_copied"), 1)
    act.activation(m.C.CT, m.pb[6][:, :].rearrange("p (n j c) -> p n j c", n=2, j=2), ACT.Copy)\
        .then_inc(m.s("s5_turned_copied"), 1)


def state_tensor(pe, m):
    pe.wait_ge(m.s("s5_turned_copied"), 2)
    pe.wait_ge(m.s("head_mean"), 5)
    for j in range(NPAIR + 2):
        if j < NPAIR:
            if j >= 2:
                pe.wait_ge(m.s("s5_mixed"), 2 * (j - 1))
            rows = slice(32 * (j % 4), 32 * (j % 4) + 32)
            u = m.C.UT[rows, j // 4, :]
            for n in range(2):
                ins = pe.matmul(m.pb[5 + j % 2][:, n * S:(n + 1) * S], m.C.BT[rows, n, j // 4, :], u,
                                start=n == 0, stop=True, skip_group_check=True, tile_position=(32 * (j % 4), 0))
            ins.then_inc(m.s("s5_inputs"), 1)
        if j >= 2:
            i = j - 2
            pe.wait_ge(m.s("s5_states"), 2 * (i + 1))
            at = slice(32 * (i % 4), 32 * (i % 4) + 32)
            out = m.pb[4][at, (i // 4) * S:(i // 4 + 1) * S]
            for n in range(2):
                ins = pe.matmul(out, m.C.CT[:, n, i // 4, at], m.C.XS[:, i % 2, n, :], start=i < 4 and n == 0,
                                stop=n == 1, skip_group_check=True, tile_position=(0, 32 * (i % 4)))
            ins.then_inc(m.s("s5_outputs"), 1)


def state_vector(dve, m):
    C = m.C
    dve.wait_ge(m.s("s5_tables"), 1)
    for j in range(NPAIR):
        dve.wait_ge(m.s("s5_inputs"), j + 1)
        bu = m.pb[5 + j % 2][:, :].rearrange("p (n t) -> p n t", n=2)
        for n, e in enumerate((C.EC, C.ES)):
            dve.tensor_tensor(C.M1[:, n], bu, e[:, j, :].unsqueeze(1).to_broadcast([P, 2, S]), ALU.mult)\
                .then_inc(m.s("s5_mixed"), 1)
        dve.wait_ge(m.s("s5_mixed"), 2 * (j + 1))
        dve.tensor_tensor(C.Z[:, 0], C.M1[:, 0, 0], C.M1[:, 1, 1], ALU.add).then_inc(m.s("s5_rotated"), 1)
        dve.tensor_tensor(C.Z[:, 1], C.M1[:, 0, 1], C.M1[:, 1, 0], ALU.subtract).then_inc(m.s("s5_rotated"), 1)
        if j >= 2:
            dve.wait_ge(m.s("s5_unmixed"), 2 * (j - 1))
        for n in range(2):
            dve.wait_ge(m.s("s5_rotated"), 2 * j + n + 1)
            dve.tensor_tensor_scan(C.SC[:, j % 2, n, :], C.MAG[:, j:j + 1].to_broadcast([P, S]), C.Z[:, n], 0.0,
                                   ALU.mult, ALU.add).then_inc(m.s("s5_scanned"), 1)
        index_round_vector(dve, m, j)
    index_choice_vector(dve, m)
    head_norms_c_vector(dve, m)
    dve.wait_ge(m.s("s5_outputs"), NPAIR)
    for jj in range(2):
        ins = dve.scalar_tensor_tensor(out=C.Y[:, jj, :], in0=C.UT[:, jj, :], scalar=C.DCOL[:, jj:jj + 1],
                                       in1=m.pb[4][:, jj * S:(jj + 1) * S], op0=ALU.mult, op1=ALU.add)
    ins.then_inc(m.s("s5g_steps"), 1)
    gelu_vector(dve, m, "s5g", C.Y, C.YT, None, C.Y)
    dve.wait_ge(m.s("s5_hi"), 1)
    dve.tensor_tensor(m.OTL[:, 4:6, :], C.Y, m.OTH[:, 4:6, :].bitcast(F32), ALU.subtract)\
        .then_inc(m.s("s5_lo"), 1)


def state_scalar(act, m):
    gelu_scalar(act, m, "s5g", m.C.YT)
    act.wait_ge(m.s("s5g_steps"), 6)
    act.activation(m.OTH[:, 4:6, :], m.C.Y, ACT.Copy).then_inc(m.s("s5_hi"), 1)


def state_gpsimd(pool, m):
    C = m.C
    for j in range(NPAIR):
        pool.wait_ge(m.s("s5_scanned"), 2 * (j + 1))
        if j >= 1:
            pool.wait_ge(m.s("s5_states"), 2 * j)
        if j >= 2:
            pool.wait_ge(m.s("s5_outputs"), j - 1)
        for n, e in enumerate((C.EC, C.ES)):
            pool.tensor_tensor(C.M3[:, n], C.SC[:, j % 2], e[:, j, :].unsqueeze(1).to_broadcast([P, 2, S]),
                               ALU.mult).then_inc(m.s("s5_unmixed"), 1)
        pool.wait_ge(m.s("s5_unmixed"), 2 * (j + 1))
        pool.tensor_tensor(C.XS[:, j % 2, 0, :], C.M3[:, 0, 0], C.M3[:, 1, 1], ALU.subtract)\
            .then_inc(m.s("s5_states"), 1)
        pool.tensor_tensor(C.XS[:, j % 2, 1, :], C.M3[:, 0, 1], C.M3[:, 1, 0], ALU.add)\
            .then_inc(m.s("s5_states"), 1)



def merge_sync(sp, m):
    n = first_unit("merge")
    w = m.i["w_in_2"][0].rearrange("(k p) n -> p k n", p=P)
    first_gate = 1476
    oa = m.i["w_o_a_2"][0].rearrange("(k p) n -> p k n", p=P)
    glu = m.i["w_glu_2"][0].rearrange("(k p) (g n) -> p k g n", p=P, g=2)
    om = m.i["w_o_m_2"][0].rearrange("(k p) n -> p k n", p=P)
    for c in range(2):
        col = slice(c * 512, (c + 1) * 512)
        for b in range(3):
            at = first_gate + b * D + c * 512
            for half in range(2):
                load_unit(sp, m, n, [(m.RAW[:, slot(n), :].rearrange("p (k c) -> p k c", k=4),
                                      w[:, 4 * half:4 * half + 4, at:at + 512])])
                n += 1
            raw = m.RAW[:, slot(n), :]
            if b == 0:
                load_unit(sp, m, n, [(raw.rearrange("p (k c) -> p k c", k=4), oa[:, :, col])])
            elif b == 1:
                v = raw.rearrange("p (k g c) -> p k g c", k=2, g=2)
                load_unit(sp, m, n, [(v[:, :, g, :], glu[:, :, g, col]) for g in range(2)])
            else:
                load_unit(sp, m, n, [(raw[:, 0:D].rearrange("p (k c) -> p k c", k=2), om[:, :, col])])
            n += 1


def merge_tensor(pe, m):
    n = first_unit("merge")
    pe.wait_ge(m.s("c_out_lo"), 6)
    pe.wait_ge(m.s("s5_lo"), 1)
    done, th, use = m.s("m_product"), m.s("m_tanh"), m.s("m_merged")
    for x in range(6):
        b = x % 3
        if x >= 2:
            pe.wait_ge(use, x - 1)
        for half in range(2):
            pe.wait_ge(m.lo_done, n + 1)
            for t in range(TT):
                tok = slice(t * P, (t + 1) * P)
                for k in range(4):
                    kt = 4 * half + k
                    at = slice(k * 512, (k + 1) * 512)
                    ins = mm3(pe, m.pb[2 * (x % 2) + t][:, :], m.HTH[:, kt, tok], m.HTL[:, kt, tok],
                              m.WH[:, slot(n), at], m.WL[:, slot(n), at], kt == 0)
            ins.then_inc(m.unit_used, 1)
            n += 1
        pe.wait_ge(m.lo_done, n + 1)
        if x >= 1:
            pe.wait_ge(use, x)
        k0, nk = ((0, 4), (4, 2), (6, 2))[b]
        for t in range(TT):
            tok = slice(t * P, (t + 1) * P)
            for k in range(nk):
                for g in range(2 if b == 1 else 1):
                    at = slice((k * 2 + g) * 512, (k * 2 + g + 1) * 512) if b == 1 else slice(k * 512, (k + 1) * 512)
                    ins = mm3(pe, m.pb[4 + 2 * g + t][:, :], m.OTH[:, k0 + k, tok], m.OTL[:, k0 + k, tok],
                              m.WH[:, slot(n), at], m.WL[:, slot(n), at], k == 0)
        ins.then_inc(m.unit_used, 1)
        n += 1
    pe.wait_ge(use, 6)
    for bank in range(4):
        for kt in (2 * bank, 2 * bank + 1):
            for t in range(TT):
                ins = pe.transpose(m.pb[bank][:, (kt % 2) * S + t * P:(kt % 2) * S + (t + 1) * P],
                                   m.C.MM[:, t, kt * P:(kt + 1) * P], m.IDENT[:, :])
        ins.then_inc(m.s("m_turned"), 1)


def merge_scalar(act, m):
    n = first_unit("merge")
    for x in range(6):
        end = n + 3 * (x + 1)
        for j in range(3):
            if x < 5 and j < 2:
                split_hi(act, m, end + j)
        act.wait_ge(m.unit_used, end)
        if x >= 1:
            act.wait_ge(m.s("m_merged"), x)
        for t in range(TT):
            act.activation(m.C.TG[:, t, :], m.pb[2 * (x % 2) + t][:, :], ACT.Tanh, scale=0.5)\
                .then_inc(m.s("m_tanh"), 1)
        if x % 3 == 1:
            for t in range(TT):
                act.activation(m.C.TB[:, t, :], m.pb[6 + t][:, :], ACT.Tanh, scale=0.5)\
                    .then_inc(m.s("m_tanh_glu"), 1)
        if x < 5:
            split_hi(act, m, end + 2)
    for bank in range(4):
        act.wait_ge(m.s("m_turned"), bank + 1)
        act.activation(m.HTH[:, 2 * bank:2 * bank + 2, :], m.pb[bank][:, :].rearrange("p (k t) -> p k t", k=2),
                       ACT.Copy, scale=0.5).then_inc(m.s("m_hi"), 1)


def merge_vector(dve, m):
    n = first_unit("merge")
    step, count = m.s("m_steps"), 0
    for x in range(6):
        c, b = x // 3, x % 3
        end = n + 3 * (x + 1)
        if x < 5:
            split_lo(dve, m, end)
            split_lo(dve, m, end + 1)
        for t in range(TT):
            mm_ = m.C.MM[:, t, c * 512:(c + 1) * 512]
            tg, tb, v = m.C.TG[:, t, :], m.C.TB[:, t, :], m.C.TV[:, t, :]
            dve.wait_ge(m.s("m_tanh"), 2 * x + t + 1)
            if b == 0:
                ins = dve.scalar_tensor_tensor(out=mm_, in0=tg, scalar=1.0, in1=m.pb[4 + t][:, :],
                                               op0=ALU.add, op1=ALU.mult)
            else:
                if b == 1:
                    dve.wait_ge(m.s("m_tanh_glu"), 2 * c + t + 1)
                    dve.scalar_tensor_tensor(out=tb, in0=tb, scalar=1.0, in1=m.pb[4 + t][:, :],
                                             op0=ALU.add, op1=ALU.mult).then_inc(step, 1)
                    count += 1
                    dve.wait_ge(step, count)
                    other, f = tb, 0.5
                else:
                    other, f = m.pb[4 + t][:, :], 1.0
                dve.scalar_tensor_tensor(out=v, in0=tg, scalar=1.0, in1=other, op0=ALU.add, op1=ALU.mult)\
                    .then_inc(step, 1)
                count += 1
                dve.wait_ge(step, count)
                ins = dve.scalar_tensor_tensor(out=mm_, in0=v, scalar=f, in1=mm_, op0=ALU.mult, op1=ALU.add)
        ins.then_inc(m.s("m_merged"), 1)
        dve.wait_ge(m.s("m_merged"), x + 1)
        if x < 5:
            split_lo(dve, m, end + 2)
    for bank in range(4):
        dve.wait_ge(m.s("m_hi"), bank + 1)
        dve.scalar_tensor_tensor(out=m.HTL[:, 2 * bank:2 * bank + 2, :].rearrange("p k t -> p (k t)"),
                                 in0=m.pb[bank][:, :], scalar=0.5,
                                 in1=m.HTH[:, 2 * bank:2 * bank + 2, :].bitcast(F32).rearrange("p k t -> p (k t)"),
                                 op0=ALU.mult, op1=ALU.subtract).then_inc(m.s("m_lo"), 1)


def mixer_out_sync(sp, m):
    n = first_unit("c_out")
    w = m.i["w_out_2"][0].rearrange("(k p) n -> p k n", p=P)
    for c in range(2):
        for half in range(2):
            load_unit(sp, m, n, [(m.RAW[:, slot(n), :].rearrange("p (k c) -> p k c", k=4),
                                  w[:, 4 * half:4 * half + 4, c * 512:(c + 1) * 512])])
            n += 1



class Cutter:

    def __init__(self, base, at):
        self.base, self.at = base, at

    def take(self, *dims):
        size = int(np.prod(dims))
        v = self.base[:, self.at:self.at + size]
        self.at += size
        assert self.at <= self.base.shape[1], (self.at, self.base.shape)
        if len(dims) == 1:
            return v
        names = "abcd"[:len(dims)]
        return v.rearrange(f"p ({' '.join(names)}) -> p {' '.join(names)}", **dict(zip(names[1:], dims[1:])))


def views(ctx, nc, m):
    def sb(name, shape, dt=F32):
        return ctx.enter_context(nc.sbuf_tensor(name, shape, dt))

    m.XR = sb("residual", [P, TT, D])
    m.HN = sb("rows", [P, TT, D])
    m.HTH, m.HTL = sb("turned_hi", [P, KT, S], F32R), sb("turned_lo", [P, KT, S], F32R)
    m.OTH, m.OTL = sb("second_hi", [P, KT, S], F32R), sb("second_lo", [P, KT, S], F32R)
    m.RAW = sb("raw_units", [P, 3, ULEN])
    m.WH, m.WL = sb("units_hi", [P, 3, ULEN], F32R), sb("units_lo", [P, 3, ULEN], F32R)
    tab = sb("tables", [P, 4096])
    arena = sb("arena", [P, 16896])
    m.IDENT, m.ONES64 = sb("ident", [P, P]), sb("ones64", [P, P])
    m.PAR, m.GC, m.HG = sb("parity", [P, 2]), sb("gain_cols", [P, 72]), sb("head_gains", [P, 4])
    m.SS, m.MS, m.RS, m.NEGHALF = (sb(x, [P, 4]) for x in ("sums", "means", "rsqrts", "neghalf"))

    rows = m.HN[:, :, :].rearrange("p t d -> p (t d)")
    cut = Cutter(rows, 0)
    m.TH = cut.take(TT, FSTEP)
    m.UU = cut.take(TT, FSTEP)
    m.GG = cut.take(TT, FSTEP)
    m.GTH = m.OTH[:, 0:2, :].rearrange("p k t -> p (k t)")
    m.GTL = m.OTL[:, 0:2, :].rearrange("p k t -> p (k t)")
    cut = Cutter(tab, 0)
    m.HOT_ = cut.take(W_ALL)
    m.TAB16_ = cut.take(W_ALL)
    m.HOTI_ = cut.take(W_IDX)
    m.TAB8_ = cut.take(W_IDX)
    m.RB_ = cut.take(HEADS)
    m.RBI_ = cut.take(8)
    m.GROW_ = cut.take(P)
    m.HOT, m.TAB16, m.HOTI, m.TAB8 = m.HOT_[0:33], m.TAB16_[0:HEADS], m.HOTI_[0:32], m.TAB8_[0:8]
    m.RB, m.RBI, m.GROW = m.RB_[0:33], m.RBI_[0:32], m.GROW_[0:72]
    cut = Cutter(tab, 0)
    m.BIAS = cut.take(HEADS, S)
    cut = Cutter(tab, 0)
    m.BIASB = cut.take(RINGB, BW)
    cut = Cutter(tab, 0)
    m.BIASC = cut.take(8, S)
    m.A = A = Names()
    cut = Cutter(arena, 0)
    A.QT = cut.take(2, 4, S)
    A.KC2 = cut.take(KV, S)
    A.VC2 = cut.take(KV, S)
    A.KST = cut.take(2, S)
    A.KWT = cut.take(2, S)
    A.VS = cut.take(TT, S)
    A.VW = cut.take(TT, S)
    A.GATE = cut.take(TT, 48)
    A.KCB = cut.take(2, 2, 16)
    A.VCR = cut.take(KV, DH)
    A.SC = cut.take(TT, HEADS, 16)
    A.CM = cut.take(TT, HEADS)
    A.CD = cut.take(TT, HEADS)
    A.GX = cut.take(S)
    A.GY = cut.take(S)
    A.GH = cut.take(2, 60)
    A.NM = cut.take(NA, 2)
    A.RS = cut.take(NA, 2)
    A.RD = cut.take(NA, 2)
    A.PE = cut.take(2, 16)
    A.W2 = cut.take(2, 2, P)
    A.BGATE = cut.take(48)
    at = cut.at
    m.PE, m.W2, m.BGATE = A.PE, A.W2, A.BGATE
    cut = Cutter(arena, at)
    A.W1K = cut.take(16, S)
    A.W1V = cut.take(16, S)
    cut = Cutter(arena, at)
    A.PB = cut.take(RINGP, 512)
    A.PT = cut.take(2, 512)
    A.PC = cut.take(TT, KV, 4, 32)
    cut = Cutter(rows, 0)
    A.RK = cut.take(16, KV, NCMP)
    A.RV = cut.take(16, KV, NCMP)
    cut = Cutter(rows, 0)
    A.HID = cut.take(2, KV, 4, 32)
    A.PCT = cut.take(KV, S)
    m.B = B = Names()
    cut = Cutter(arena, 0)
    B.QT = cut.take(3, 2, 4, S)
    B.KT = cut.take(3, 2, S)
    B.V = cut.take(3, TT, S)
    B.PB = cut.take(RINGP, 512)
    B.PT = cut.take(2, 512)
    B.NM = cut.take(NB)
    B.RS = cut.take(NB)
    B.RD = cut.take(NB)
    m.C = C = Names()
    cut = Cutter(arena, 0)
    C.LR = cut.take(NPAIR)
    C.LI = cut.take(NPAIR)
    C.DT = cut.take(NPAIR)
    C.MAG = cut.take(NPAIR)
    C.SIN = cut.take(NPAIR)
    C.COS = cut.take(NPAIR)
    C.T = cut.take(11, NPAIR)
    C.DCOL = cut.take(2)
    C.HGS = cut.take(2)
    C.EC = cut.take(NPAIR, S)
    C.ES = cut.take(NPAIR, S)
    C.BT = cut.take(2, 2, P)
    C.CT = cut.take(2, 2, P)
    C.MKT = cut.take(2 * S)
    C.MV = cut.take(TT, S)
    C.QMR = cut.take(2 * S)
    C.KI = cut.take(S)
    C.VA = cut.take(TT, DH)
    C.WI = cut.take(TT, 4)
    C.UT = cut.take(2, S)
    C.ZERO = cut.take(S)
    C.NM = cut.take(NC, 2)
    C.RS = cut.take(NC, 2)
    C.RD = cut.take(NC, 2)
    at = cut.at
    cut = Cutter(arena, at)
    C.BN = cut.take(2, NPAIR, 16)
    C.BW = cut.take(2, NPAIR, 16)
    C.BX = cut.take(2, NPAIR, 32)
    C.CN = cut.take(2, 2, P)
    cut = Cutter(arena, at)
    C.QR = cut.take(2, 2 * S)
    C.KR = cut.take(S)
    C.QI = cut.take(2, S)
    at = cut.at
    cut = Cutter(arena, at)
    m.GB = cut.take(D)
    cut = Cutter(arena, at)
    C.IS = cut.take(S + P)
    C.SM = cut.take(S + P)
    C.TOP = cut.take(2, 8)
    C.BM = cut.take(2, S + P)
    at = cut.at
    cut = Cutter(arena, at)
    C.M1 = cut.take(2, 2, S)
    C.Z = cut.take(2, S)
    C.SC = cut.take(2, 2, S)
    C.M3 = cut.take(2, 2, S)
    C.XS = cut.take(2, 2, S)
    cut = Cutter(arena, at)
    C.Y = cut.take(2, S)
    C.YT = cut.take(2, S)
    cut = Cutter(arena, at)
    C.ET = cut.take(2, NPAIR, P)
    cut = Cutter(arena, at)
    C.MEM = cut.take(TT, D)
    C.SQMK = cut.take(2 * S)
    C.MSMK = cut.take(2 * S)
    cut = Cutter(arena, at)
    C.PB = cut.take(RINGP, 512)
    C.PT = cut.take(2, 512)
    cut = Cutter(arena, at)
    C.TG = cut.take(TT, 512)
    C.TB = cut.take(TT, 512)
    C.TV = cut.take(TT, 512)
    cut = Cutter(rows, 0)
    C.SQ = cut.take(2, 2 * S)
    C.MS2 = cut.take(2, 2 * S)
    cut = Cutter(rows, 0)
    C.RL = cut.take(4, S + P)
    cut = Cutter(rows, 0)
    C.MM = cut.take(TT, D)
    cut = Cutter(tab, 8 * S)
    C.SQM = cut.take(2 * S)
    C.MSM = cut.take(2 * S)
    C.SQK = cut.take(S)
    C.MSK = cut.take(S)
    C.MKR, C.QM, C.QT, C.KT = C.MKT, C.QMR, C.QR, C.KR


def hybrid_transformer_kernel(nc, i, out):
    with ExitStack() as ctx:
        m = Names()
        m.i, m.n_consts, m.ncmp = i, 23, (7, NCMP)
        views(ctx, nc, m)
        m.pb = [ctx.enter_context(nc.psum_tensor(f"bank{b}", [P, 512], F32)) for b in range(8)]
        m.TD = nc.dram_tensor("distance_tables", [2, HEADS, W_ALL], F32, kind="Internal").ap()
        m.TDI = nc.dram_tensor("index_distance_table", [2, 8, W_IDX], F32, kind="Internal").ap()

        sems = {}

        def semaphore(name):
            if name not in sems:
                sems[name] = ctx.enter_context(nc.semaphore(name))
            return sems[name]

        m.s = semaphore
        m.raw_landed = [semaphore(f"raw_landed{k}") for k in range(3)]
        m.bias_b_in = [semaphore(f"bias_b_in{k}") for k in range(RINGB)]
        m.hi_done, m.lo_done, m.unit_used = (semaphore(x) for x in ("hi_done", "lo_done", "unit_used"))
        m.x_ready, m.consts_in = semaphore("x_ready"), semaphore("consts_in")
        ctx.enter_context(nc.allow_non_contiguous_dma(reason="small parameter columns"))
        block = ctx.enter_context(nc.Block())

        def x_after(n):
            return m.x_ready, 2 * n - 1, 1

        HT, OT = (m.HTH, m.HTL), (m.OTH, m.OTL)

        @block.sync
        def _(sp):
            first_loads_sync(sp, m)
            project_a_sync(sp, m)
            out_sync(sp, m, "a_out", i["a_w_out"][0])
            ffn_sync(sp, m, 0, i["ffn_w_up"][0], i["ffn_w_down"][0])
            bias_b_sync(sp, m, range(RINGB))
            project_b_sync(sp, m)
            out_sync(sp, m, "b_out", i["b_w_out"][0], 0, 3)
            bias_b_sync(sp, m, range(RINGB, NB // 2))
            out_sync(sp, m, "b_out", i["b_w_out"][0], 3, 4)
            ffn_sync(sp, m, 1, i["ffn_w_up"][1], i["ffn_w_down"][1])
            ffn_sync(sp, m, 2, i["ffn1_w_in_2"][0], i["ffn1_w_out_2"][0])
            memory_sync(sp, m)
            project_c_sync(sp, m)
            merge_sync(sp, m)
            mixer_out_sync(sp, m)
            ffn_sync(sp, m, 3, i["ffn2_w_in_2"][0], i["ffn2_w_out_2"][0])
            for t in range(TT):
                sp.wait_ge(m.s("result_ready"), t + 1)
                sp.dma_start(out[0, t * P:(t + 1) * P, :], m.XR[:, t, :]).then_inc(m.s("stored"), 16)
            sp.wait_ge(m.s("stored"), 16 * TT)

        @block.gpsimd
        def _(pool):
            pool.wait_ge(m.s("neghalf_set"), 2)
            norm_gpsimd(pool, m, 0)
            setup_dma(pool, m)
            tables_gpsimd(pool, m)
            compress_gpsimd(pool, m)
            norm_gpsimd(pool, m, 1)
            norm_gpsimd(pool, m, 2)
            pool.wait_ge(m.s("b_biased"), NB)
            for h in range(8):
                pool.dma_start(m.BIASC[:, h, :], sliding(m.TDI, h * W_IDX + 127, 1, [[1, S]]))\
                    .then_inc(m.s("bias_c_in"), 16)
            norm_gpsimd(pool, m, 3)
            state_loads_gpsimd(pool, m, (m.x_ready, 2 * 3))
            row_norm_gpsimd(pool, m, 0, (m.x_ready, 2 * 3), i["final_norm"])
            norm_gpsimd(pool, m, 4)
            state_params_gpsimd(pool, m)
            state_tables_gpsimd(pool, m)
            pool.dma_start(m.C.MEM, i["mem_2"][0].rearrange("(t p) d -> p t d", p=P)).then_inc(m.s("mem_in"), 16)
            norm_gpsimd(pool, m, 5)
            norm_gpsimd(pool, m, 6)
            pool.memset(m.C.ZERO, 0.0).then_inc(m.s("zero_set"), 1)
            state_gpsimd(pool, m)
            attend_c_gpsimd(pool, m)
            norm_gpsimd(pool, m, 7)
            row_norm_gpsimd(pool, m, 1, (m.x_ready, 2 * 7), i["final_norm_2"])

        @block.scalar
        def _(act):
            norm_squares_scalar(act, m, m.XR, (m.s("x_in"), 16, 0), None)
            split_ahead(act, m, split_hi, "a_in", 0, 1)
            norm_turned_scalar(act, m, 0, [(m.HTH, m.HTL, 0)], gains=True)
            split_ahead(act, m, split_hi, "a_in", 1, 2)
            project_a_scalar(act, m)
            split_ahead(act, m, split_hi, "a_out", 0, 3)
            compress_scalar(act, m)
            attend_a_scalar(act, m)
            split_ahead(act, m, split_hi, "a_out", 3, 4)
            norm_scalar(act, m, 1, m.XR, [(m.HTH, m.HTL, 1)], x_after(1), "ffn0")
            ffn_scalar(act, m, 0)
            norm_scalar(act, m, 2, m.XR, [(m.HTH, m.HTL, 2), (m.OTH, m.OTL, 3)], x_after(2), "b_in")
            project_b_scalar(act, m)
            split_ahead(act, m, split_hi, "b_out", 0, 1)
            attend_b_scalar(act, m)
            split_ahead(act, m, split_hi, "b_out", 1, 3)
            split_ahead(act, m, split_hi, "b_out", 3, 4)
            norm_scalar(act, m, 3, m.XR, [(m.HTH, m.HTL, 4)], x_after(3), "ffn1")
            ffn_scalar(act, m, 1)
            split_ahead(act, m, split_hi, "ffn2", 0, 2)
            row_norm_scalar(act, m, 0, x_after(4))
            state_step_scalar(act, m)
            norm_scalar(act, m, 4, m.XR, [(m.HTH, m.HTL, 5)], x_after(5), None)
            state_functions_scalar(act, m)
            ffn_scalar(act, m, 2)
            norm_scalar(act, m, 5, m.C.MEM, [(m.HTH, m.HTL, 6)], (m.s("mem_in"), 16, 0), "mem_kv")
            state_turn_scalar(act, m)
            norm_squares_scalar(act, m, m.XR, x_after(6), None)
            memory_scalar(act, m)
            split_ahead(act, m, split_hi, "c_in", 0, 2)
            norm_turned_scalar(act, m, 6, [(m.HTH, m.HTL, 7)])
            project_c_scalar(act, m)
            index_scalar(act, m)
            state_scalar(act, m)
            split_ahead(act, m, split_hi, "merge", 0, 1)
            attend_c_scalar(act, m)
            split_ahead(act, m, split_hi, "merge", 1, 3)
            merge_scalar(act, m)
            split_ahead(act, m, split_hi, "c_out", 0, 4)
            norm_scalar(act, m, 7, m.XR, [(m.HTH, m.HTL, 8)], x_after(7), "ffn3")
            ffn_scalar(act, m, 3)
            row_norm_scalar(act, m, 1, x_after(8))

        @block.vector
        def _(dve):
            setup_vector(dve, m)
            norm_scale_vector(dve, m, 0, m.XR)
            split_ahead(dve, m, split_lo, "a_in", 0, 1)
            norm_turned_vector(dve, m, 0, [(m.HTH, m.HTL, 0)])
            split_ahead(dve, m, split_lo, "a_in", 1, 2)
            project_a_vector(dve, m)
            split_ahead(dve, m, split_lo, "a_out", 0, 3)
            compress_vector(dve, m)
            attend_a_vector(dve, m)
            split_ahead(dve, m, split_lo, "a_out", 3, 4)
            residual(dve, m, "a_out", 1.0, "ffn0")
            norm_vector(dve, m, 1, m.XR, [(m.HTH, m.HTL, 1)])
            ffn_vector(dve, m, 0, 0.5, "b_in")
            norm_vector(dve, m, 2, m.XR, [(m.HTH, m.HTL, 2), (m.OTH, m.OTL, 3)])
            project_b_vector(dve, m)
            split_ahead(dve, m, split_lo, "b_out", 0, 1)
            attend_b_vector(dve, m)
            split_ahead(dve, m, split_lo, "b_out", 1, 3)
            split_ahead(dve, m, split_lo, "b_out", 3, 4)
            residual(dve, m, "b_out", 1.0, "ffn1")
            norm_vector(dve, m, 3, m.XR, [(m.HTH, m.HTL, 4)])
            ffn_vector(dve, m, 1, 0.5, "ffn2")
            row_norm_vector(dve, m, 0, m.x_ready)
            norm_vector(dve, m, 4, m.XR, [(m.HTH, m.HTL, 5)])
            ffn_vector(dve, m, 2, 0.25, "mem_kv")
            norm_vector(dve, m, 5, m.C.MEM, [(m.HTH, m.HTL, 6)])
            norm_scale_vector(dve, m, 6, m.XR)
            memory_vector(dve, m)
            split_ahead(dve, m, split_lo, "c_in", 0, 2)
            norm_turned_vector(dve, m, 6, [(m.HTH, m.HTL, 7)])
            project_c_vector(dve, m)
            index_scores_vector(dve, m)
            state_vector(dve, m)
            split_ahead(dve, m, split_lo, "merge", 0, 1)
            dve.wait_ge(m.s("zero_set"), 1)
            dve.wait_ge(m.s("s5_lo"), 1)
            attend_c_vector(dve, m)
            split_ahead(dve, m, split_lo, "merge", 1, 3)
            merge_vector(dve, m)
            split_ahead(dve, m, split_lo, "c_out", 0, 4)
            residual(dve, m, "c_out", 1.0, "ffn3")
            norm_vector(dve, m, 7, m.XR, [(m.HTH, m.HTL, 8)])
            ffn_vector(dve, m, 3, 0.25)
            row_norm_vector(dve, m, 1, m.s("result_ready"))

        @block.tensor
        def _(pe):
            setup_tensor(pe, m)
            norm_tensor(pe, m, 0)
            project_a_tensor(pe, m)
            compress_tensor(pe, m)
            attend_a_tensor(pe, m)
            out_tensor(pe, m, "a_out", OT, (m.s("a_out_lo"), 8))
            norm_tensor(pe, m, 1)
            ffn_tensor(pe, m, 0, 1)
            norm_tensor(pe, m, 2)
            project_b_tensor(pe, m)
            attend_b_tensor(pe, m)
            out_tensor(pe, m, "b_out", OT, (m.s("b_out_lo"), 8))
            norm_tensor(pe, m, 3)
            ffn_tensor(pe, m, 1, 3)
            norm_tensor(pe, m, 4)
            ffn_tensor(pe, m, 2, 4)
            norm_tensor(pe, m, 5)
            state_turn_tensor(pe, m)
            memory_tensor(pe, m)
            pe.wait_ge(m.s("mk_raw"), 1)
            pe.wait_ge(m.s("mv_ready"), 1)
            norm_tensor(pe, m, 6)
            project_c_tensor(pe, m)
            index_tensor(pe, m)
            state_tensor(pe, m)
            attend_c_tensor(pe, m)
            merge_tensor(pe, m)
            out_tensor(pe, m, "c_out", HT, (m.s("m_lo"), 4))
            norm_tensor(pe, m, 7)
            ffn_tensor(pe, m, 3, 7)


def split_ahead(eng, m, split, stage, first, last):
    for j in range(first, last):
        split(eng, m, first_unit(stage) + j)


def residual(dve, m, stage, factor, following):
    split_ahead(dve, m, split_lo, following, 0, 2)
    add_residual(dve, m, factor, {"a_out": 0, "b_out": 2, "c_out": 5}[stage], first_unit(stage) + 3)


_INS = ['x', 'rel_bias', 'norm_mix', 'norm_ffn', 'a_w_in', 'a_b_gate', 'a_pe_k', 'a_w1_k', 'a_w2_k', 'a_pe_v',
        'a_w1_v', 'a_w2_v', 'a_w_out', 'kv_norm', 'kv_w', 'b_w_q', 'b_w_out', 'ffn_w_up', 'ffn_w_down',
        'final_norm', 'mem_2', 'ffn1_norm_2', 'ffn1_w_in_2', 'ffn1_w_out_2', 'mix_norm_2', 'w_in_2',
        'a_q_gain_2', 'a_k_gain_2', 'rel_bias_2', 'w_o_a_2', 'ssm_lambda_re_2', 'ssm_lambda_im_2',
        'ssm_log_dt_2', 'ssm_b_re_2', 'ssm_b_im_2', 'ssm_c_re_2', 'ssm_c_im_2', 'ssm_d_2', 'w_glu_2',
        'mem_norm_2', 'w_mem_kv_2', 'm_q_gain_2', 'm_k_gain_2', 'w_o_m_2', 'w_out_2', 'ffn2_norm_2',
        'ffn2_w_in_2', 'ffn2_w_out_2', 'final_norm_2']


def kernel(**inputs):
    import numpy as _np
    import concourse.bacc as _bacc
    from concourse import mybir as _mybir
    from concourse.bass_utils import run_bass_kernel_spmd as _run

    nc = _bacc.Bacc("TRN2", target_bir_lowering=False, num_devices=1)
    arrays, handles = {}, {}
    for name, a in [(n, inputs[n]) for n in _INS] + list(shape_constants().items()):
        a = _np.ascontiguousarray(a)
        arrays[f"in_{name}"] = a
        handles[name] = nc.dram_tensor(f"in_{name}", a.shape, _mybir.dt.from_np(a.dtype),
                                                kind="ExternalInput").ap()
    out = nc.dram_tensor("out_0", (1, S, D), F32, kind="ExternalOutput").ap()
    hybrid_transformer_kernel(nc, handles, out)
    r = _run(nc, [arrays], core_ids=[0])
    return r.results[0]["out_0"]
```
